# Optimizing a Trainium2 kernel written in Bass

```python
import math
import jax, jax.numpy as jnp
from jax import lax
import numpy as np

D_MODEL = 1024
BATCH = 1
SEQ = 1024
DEPTH = 1
DEC_BATCH = 8
DEC_SEQ = 8
PAST_LEN = 8192
PAGE_SIZE = 128

D_MIX = D_MODEL
D_S5 = D_MIX // 2
D_LRU = D_MIX - D_S5
S5_GROUP = 16
S5_GROUPS = D_S5 // S5_GROUP
S5_STATE = 64
LRU_HEADS = 8
LRU_HEAD_DIM = D_LRU // LRU_HEADS
CONV_W = 4
LRU_C = 8.0
N_MEM = 256
XA_HEADS = 4
XA_HEAD_DIM = D_MODEL // XA_HEADS
N_EXPERT_GROUPS = 4
EXPERTS_PER_GROUP = 8
N_EXPERTS = N_EXPERT_GROUPS * EXPERTS_PER_GROUP
TOP_K_IN_GROUP = 2
D_FF_EXPERT = D_MODEL // 4
EPS = 1e-6

kernel_name = "hymba_s5_rglru_hiermoe_step"

def _rmsnorm(x, g):
    xf = x.astype(jnp.float32)
    y = xf * lax.rsqrt(jnp.mean(xf * xf, axis=-1, keepdims=True) + EPS)
    return (y * g.astype(jnp.float32)).astype(x.dtype)

def _complex_diag_combine(e1, e2):
    a1r, a1i, b1r, b1i = e1
    a2r, a2i, b2r, b2i = e2
    return (a2r * a1r - a2i * a1i,
            a2r * a1i + a2i * a1r,
            a2r * b1r - a2i * b1i + b2r,
            a2r * b1i + a2i * b1r + b2i)

def _real_diag_combine(e1, e2):
    a1, b1 = e1
    a2, b2 = e2
    return a2 * a1, a2 * b1 + b2

def _s5(u, h0_re, h0_im, lam_re, lam_im, log_dt, b_re, b_im, c_re, c_im, d_skip, w_glu, b_glu):
    f32 = jnp.float32
    bsz, s, _ = u.shape
    uf = u.astype(f32).reshape(bsz, s, S5_GROUPS, S5_GROUP)
    lr = lam_re.astype(f32)
    li = lam_im.astype(f32)
    dt = jnp.exp(log_dt.astype(f32))[:, None]
    mag = jnp.exp(lr * dt)
    ab_re = mag * jnp.cos(li * dt)
    ab_im = mag * jnp.sin(li * dt)
    den = lr * lr + li * li
    nr = ab_re - 1.0
    f_re = (nr * lr + ab_im * li) / den
    f_im = (ab_im * lr - nr * li) / den
    br = b_re.astype(f32)
    bi = b_im.astype(f32)
    bb_re = f_re[..., None] * br - f_im[..., None] * bi
    bb_im = f_re[..., None] * bi + f_im[..., None] * br
    bu_re = jnp.einsum("bsgc,gnc->bsgn", uf, bb_re)
    bu_im = jnp.einsum("bsgc,gnc->bsgn", uf, bb_im)
    h0r = h0_re.astype(f32)
    h0i = h0_im.astype(f32)
    bu_re = bu_re.at[:, 0].add(ab_re * h0r - ab_im * h0i)
    bu_im = bu_im.at[:, 0].add(ab_re * h0i + ab_im * h0r)
    a_re = jnp.broadcast_to(ab_re, bu_re.shape)
    a_im = jnp.broadcast_to(ab_im, bu_im.shape)
    _, _, h_re, h_im = lax.associative_scan(_complex_diag_combine, (a_re, a_im, bu_re, bu_im), axis=1)
    y = (jnp.einsum("bsgn,gcn->bsgc", h_re, c_re.astype(f32))
         - jnp.einsum("bsgn,gcn->bsgc", h_im, c_im.astype(f32))
         + d_skip.astype(f32) * uf)
    y = jax.nn.gelu(y.reshape(bsz, s, D_S5)).astype(u.dtype)
    out = y * jax.nn.sigmoid(y @ w_glu + b_glu)
    return out, h_re[:, -1], h_im[:, -1]

def _rglru(xb, gb, h0, conv_buf, conv_w, conv_b, w_a, b_a, w_x, b_x, lam):
    f32 = jnp.float32
    bsz, s, _ = xb.shape
    xp = jnp.concatenate([conv_buf.astype(xb.dtype), xb], axis=1)
    xc = conv_b + xp[:, 0:s] * conv_w[0]
    for k in range(1, CONV_W):
        xc = xc + xp[:, k:k + s] * conv_w[k]
    new_buf = xp[:, s:]
    xcf = xc.astype(f32)
    xh = xcf.reshape(bsz, s, LRU_HEADS, LRU_HEAD_DIM)
    r = jax.nn.sigmoid(jnp.einsum("bshi,hij->bshj", xh, w_a.astype(f32)) + b_a.astype(f32)).reshape(bsz, s, D_LRU)
    ig = jax.nn.sigmoid(jnp.einsum("bshi,hij->bshj", xh, w_x.astype(f32)) + b_x.astype(f32)).reshape(bsz, s, D_LRU)
    log_a = -LRU_C * r * jax.nn.softplus(-lam.astype(f32))
    a = jnp.exp(log_a)
    b = jnp.sqrt(-jnp.expm1(2.0 * log_a)) * (ig * xcf)
    b = b.at[:, 0].add(a[:, 0] * h0.astype(f32))
    _, h = lax.associative_scan(_real_diag_combine, (a, b), axis=1)
    y = (h * jax.nn.gelu(gb.astype(f32))).astype(xb.dtype)
    return y, h[:, -1], new_buf

def _mem_kv(mem, g_mem, w_k, w_v):
    bsz = mem.shape[0]
    m = _rmsnorm(mem, g_mem)
    k = (m @ w_k).reshape(bsz, N_MEM, XA_HEADS, XA_HEAD_DIM)
    v = (m @ w_v).reshape(bsz, N_MEM, XA_HEADS, XA_HEAD_DIM)
    return k, v

def _cross_attend(x, mem_k, mem_v, g, w_q, w_o):
    bsz, s, _ = x.shape
    h = _rmsnorm(x, g)
    q = (h @ w_q).reshape(bsz, s, XA_HEADS, XA_HEAD_DIM).astype(jnp.float32)
    sc = jnp.einsum("bshd,bmhd->bhsm", q, mem_k.astype(jnp.float32)) * (XA_HEAD_DIM ** -0.5)
    p = jax.nn.softmax(sc, axis=-1)
    o = jnp.einsum("bhsm,bmhd->bshd", p, mem_v.astype(jnp.float32)).reshape(bsz, s, D_MODEL)
    return o.astype(x.dtype) @ w_o

def _hier_moe(x, g, w_group, w_expert, w_gate, w_up, w_down):
    f32 = jnp.float32
    bsz, s, _ = x.shape
    hf = _rmsnorm(x, g).reshape(bsz * s, D_MODEL)
    lg = (hf @ w_group).astype(f32)
    pg = jax.nn.softmax(lg, axis=-1)
    _, gsel = lax.top_k(lg, 1)
    g_onehot = jax.nn.one_hot(gsel[:, 0], N_EXPERT_GROUPS, dtype=f32)
    pg_sel = jnp.sum(pg * g_onehot, axis=-1, keepdims=True)
    le = (hf @ w_expert).astype(f32).reshape(-1, N_EXPERT_GROUPS, EXPERTS_PER_GROUP)
    le_sel = jnp.einsum("tge,tg->te", le, g_onehot)
    top_v, top_i = lax.top_k(le_sel, TOP_K_IN_GROUP)
    gate_w = jax.nn.softmax(top_v, axis=-1) * pg_sel
    expert_id = gsel * EXPERTS_PER_GROUP + top_i
    combine = jnp.sum(jax.nn.one_hot(expert_id, N_EXPERTS, dtype=f32) * gate_w[..., None], axis=1)
    act = jax.nn.silu(jnp.einsum("td,edf->tef", hf, w_gate)) * jnp.einsum("td,edf->tef", hf, w_up)
    out = jnp.einsum("tef,efd->td", act * combine[..., None].astype(act.dtype), w_down)
    return out.reshape(bsz, s, D_MODEL).astype(x.dtype)

def _layer(x, mem_k, mem_v, s5_re, s5_im, lru_h, lru_conv, w):
    h = _rmsnorm(x, w["g_mix"])
    proj = h @ w["w_in"]
    u_s5 = proj[..., :D_S5]
    x_lru = proj[..., D_S5:D_S5 + D_LRU]
    g_lru = proj[..., D_S5 + D_LRU:]
    y_s5, s5_re_n, s5_im_n = _s5(u_s5, s5_re, s5_im, w["s5_lam_re"], w["s5_lam_im"], w["s5_log_dt"],
                                 w["s5_b_re"], w["s5_b_im"], w["s5_c_re"], w["s5_c_im"], w["s5_d"],
                                 w["s5_w_glu"], w["s5_b_glu"])
    y_lru, lru_h_n, lru_conv_n = _rglru(x_lru, g_lru, lru_h, lru_conv, w["lru_conv_w"], w["lru_conv_b"],
                                        w["lru_w_a"], w["lru_b_a"], w["lru_w_x"], w["lru_b_x"], w["lru_lam"])
    x = x + jnp.concatenate([y_s5, y_lru], axis=-1) @ w["w_out"]
    x = x + _cross_attend(x, mem_k, mem_v, w["g_xa"], w["xa_w_q"], w["xa_w_o"])
    x = x + _hier_moe(x, w["g_moe"], w["moe_w_group"], w["moe_w_expert"], w["moe_w_gate"], w["moe_w_up"], w["moe_w_down"])
    return x, s5_re_n, s5_im_n, lru_h_n, lru_conv_n

def setup_inputs(seed: int = 0) -> dict:
    key = jax.random.key(seed)
    ks = iter(jax.random.split(key, 64))
    f32 = jnp.float32
    L = DEPTH

    def nrm(shape, scale):
        return scale * jax.random.normal(next(ks), shape, f32)

    n_idx = jnp.arange(S5_STATE, dtype=f32)
    a_c = jax.random.uniform(next(ks), (L, D_LRU), f32, 0.9, 0.999)
    a_base = a_c ** (1.0 / LRU_C)
    return {
        "x_prompt": nrm((BATCH, SEQ, D_MODEL), 1.0),
        "x_sample": nrm((DEC_BATCH, DEC_SEQ, D_MODEL), 1.0),
        "mem_prompt": nrm((BATCH, N_MEM, D_MODEL), 1.0),
        "cache_mem_k": nrm((L, DEC_BATCH, N_MEM, XA_HEADS, XA_HEAD_DIM), 1.0),
        "cache_mem_v": nrm((L, DEC_BATCH, N_MEM, XA_HEADS, XA_HEAD_DIM), 1.0),
        "state_s5_re": nrm((L, DEC_BATCH, S5_GROUPS, S5_STATE), 0.3),
        "state_s5_im": nrm((L, DEC_BATCH, S5_GROUPS, S5_STATE), 0.3),
        "state_lru_h": nrm((L, DEC_BATCH, D_LRU), 0.5),
        "state_lru_conv": nrm((L, DEC_BATCH, CONV_W - 1, D_LRU), 1.0),
        "g_mix": 1.0 + nrm((L, D_MODEL), 0.02),
        "w_in": nrm((L, D_MODEL, D_S5 + 2 * D_LRU), D_MODEL ** -0.5),
        "s5_lam_re": -0.5 + nrm((L, S5_GROUPS, S5_STATE), 0.01),
        "s5_lam_im": math.pi * n_idx + nrm((L, S5_GROUPS, S5_STATE), 0.01),
        "s5_log_dt": jax.random.uniform(next(ks), (L, S5_GROUPS), f32, math.log(1e-3), math.log(1e-1)),
        "s5_b_re": nrm((L, S5_GROUPS, S5_STATE, S5_GROUP), (2 * S5_GROUP) ** -0.5),
        "s5_b_im": nrm((L, S5_GROUPS, S5_STATE, S5_GROUP), (2 * S5_GROUP) ** -0.5),
        "s5_c_re": nrm((L, S5_GROUPS, S5_GROUP, S5_STATE), (2 * S5_STATE) ** -0.5),
        "s5_c_im": nrm((L, S5_GROUPS, S5_GROUP, S5_STATE), (2 * S5_STATE) ** -0.5),
        "s5_d": nrm((L, S5_GROUPS, S5_GROUP), 1.0),
        "s5_w_glu": nrm((L, D_S5, D_S5), D_S5 ** -0.5),
        "s5_b_glu": nrm((L, D_S5), 0.02),
        "lru_conv_w": nrm((L, CONV_W, D_LRU), CONV_W ** -0.5),
        "lru_conv_b": nrm((L, D_LRU), 0.02),
        "lru_w_a": nrm((L, LRU_HEADS, LRU_HEAD_DIM, LRU_HEAD_DIM), LRU_HEAD_DIM ** -0.5),
        "lru_b_a": nrm((L, LRU_HEADS, LRU_HEAD_DIM), 0.02),
        "lru_w_x": nrm((L, LRU_HEADS, LRU_HEAD_DIM, LRU_HEAD_DIM), LRU_HEAD_DIM ** -0.5),
        "lru_b_x": nrm((L, LRU_HEADS, LRU_HEAD_DIM), 0.02),
        "lru_lam": jnp.log(a_base) - jnp.log1p(-a_base),
        "w_out": nrm((L, D_MIX, D_MODEL), D_MIX ** -0.5),
        "g_xa": 1.0 + nrm((L, D_MODEL), 0.02),
        "g_mem": 1.0 + nrm((L, D_MODEL), 0.02),
        "xa_w_q": nrm((L, D_MODEL, D_MODEL), D_MODEL ** -0.5),
        "xa_w_k": nrm((L, D_MODEL, D_MODEL), D_MODEL ** -0.5),
        "xa_w_v": nrm((L, D_MODEL, D_MODEL), D_MODEL ** -0.5),
        "xa_w_o": nrm((L, D_MODEL, D_MODEL), D_MODEL ** -0.5),
        "g_moe": 1.0 + nrm((L, D_MODEL), 0.02),
        "moe_w_group": nrm((L, D_MODEL, N_EXPERT_GROUPS), D_MODEL ** -0.5),
        "moe_w_expert": nrm((L, D_MODEL, N_EXPERTS), D_MODEL ** -0.5),
        "moe_w_gate": nrm((L, N_EXPERTS, D_MODEL, D_FF_EXPERT), D_MODEL ** -0.5),
        "moe_w_up": nrm((L, N_EXPERTS, D_MODEL, D_FF_EXPERT), D_MODEL ** -0.5),
        "moe_w_down": nrm((L, N_EXPERTS, D_FF_EXPERT, D_MODEL), D_FF_EXPERT ** -0.5),
        "g_final": 1.0 + nrm((D_MODEL,), 0.02),
    }

def reference(x_prompt, x_sample, mem_prompt, cache_mem_k, cache_mem_v, state_s5_re, state_s5_im,
              state_lru_h, state_lru_conv, g_mix, w_in, s5_lam_re, s5_lam_im, s5_log_dt, s5_b_re, s5_b_im,
              s5_c_re, s5_c_im, s5_d, s5_w_glu, s5_b_glu, lru_conv_w, lru_conv_b, lru_w_a, lru_b_a, lru_w_x,
              lru_b_x, lru_lam, w_out, g_xa, g_mem, xa_w_q, xa_w_k, xa_w_v, xa_w_o, g_moe, moe_w_group,
              moe_w_expert, moe_w_gate, moe_w_up, moe_w_down, g_final):
    f32 = jnp.float32
    xp = x_prompt
    xs = x_sample
    mk_p, mv_p = [], []
    s5r_p, s5i_p, lh_p, lc_p = [], [], [], []
    s5r_s, s5i_s, lh_s, lc_s = [], [], [], []
    for l in range(DEPTH):
        w = {
            "g_mix": g_mix[l], "w_in": w_in[l],
            "s5_lam_re": s5_lam_re[l], "s5_lam_im": s5_lam_im[l], "s5_log_dt": s5_log_dt[l],
            "s5_b_re": s5_b_re[l], "s5_b_im": s5_b_im[l], "s5_c_re": s5_c_re[l], "s5_c_im": s5_c_im[l],
            "s5_d": s5_d[l], "s5_w_glu": s5_w_glu[l], "s5_b_glu": s5_b_glu[l],
            "lru_conv_w": lru_conv_w[l], "lru_conv_b": lru_conv_b[l], "lru_w_a": lru_w_a[l],
            "lru_b_a": lru_b_a[l], "lru_w_x": lru_w_x[l], "lru_b_x": lru_b_x[l], "lru_lam": lru_lam[l],
            "w_out": w_out[l], "g_xa": g_xa[l], "xa_w_q": xa_w_q[l], "xa_w_o": xa_w_o[l],
            "g_moe": g_moe[l], "moe_w_group": moe_w_group[l], "moe_w_expert": moe_w_expert[l],
            "moe_w_gate": moe_w_gate[l], "moe_w_up": moe_w_up[l], "moe_w_down": moe_w_down[l],
        }
        mk, mv = _mem_kv(mem_prompt, g_mem[l], xa_w_k[l], xa_w_v[l])
        zr = jnp.zeros((BATCH, S5_GROUPS, S5_STATE), f32)
        zh = jnp.zeros((BATCH, D_LRU), f32)
        zc = jnp.zeros((BATCH, CONV_W - 1, D_LRU), xp.dtype)
        xp, a1, a2, a3, a4 = _layer(xp, mk, mv, zr, zr, zh, zc, w)
        mk_p.append(mk)
        mv_p.append(mv)
        s5r_p.append(a1)
        s5i_p.append(a2)
        lh_p.append(a3)
        lc_p.append(a4)
        xs, b1, b2, b3, b4 = _layer(xs, cache_mem_k[l], cache_mem_v[l], state_s5_re[l], state_s5_im[l],
                                    state_lru_h[l], state_lru_conv[l], w)
        s5r_s.append(b1)
        s5i_s.append(b2)
        lh_s.append(b3)
        lc_s.append(b4)
    y_prompt = _rmsnorm(xp, g_final)
    y_sample = _rmsnorm(xs, g_final)
    return (y_prompt, y_sample,
            jnp.stack(mk_p), jnp.stack(mv_p),
            jnp.stack(s5r_p), jnp.stack(s5i_p), jnp.stack(lh_p), jnp.stack(lc_p),
            jnp.stack(s5r_s), jnp.stack(s5i_s), jnp.stack(lh_s), jnp.stack(lc_s))


_drawn_inputs = setup_inputs


def setup_inputs(seed=0):
    import zlib

    import numpy as np

    out = dict(_drawn_inputs(seed))
    spreads = {}
    factors = {'s5_lam_re': 17.917,
     's5_b_glu': 7.094,
     'lru_b_a': 8.0,
     'lru_b_x': 8.0,
     'g_xa': 5.526,
     'g_mem': 2.76,
     'g_final': 8.353,
     'g_moe': 2.685}
    for name, (base, spread) in spreads.items():
        noise = np.random.default_rng([zlib.crc32(name.encode()), seed]).standard_normal(out[name].shape)
        drawn = base * np.exp(spread * noise) if base else spread * noise
        out[name] = __import__('jax').numpy.asarray(drawn.astype(out[name].dtype))
    for name, factor in factors.items():
        out[name] = (out[name] * factor).astype(out[name].dtype)
    return out
```

```python
import math
from contextlib import ExitStack

import concourse.bass as bass
from concourse import mybir

D = 1024
P = 128
KD = D // P
SEQ = 1024
NB, DS = 8, 8
TOK = SEQ + NB * DS
NT = (TOK + P - 1) // P
ROWS = [min(P, TOK - i * P) for i in range(NT)]
CHUNKS = [(0, 512), (512, 512), (1024, TOK - 1024)]
DH = 512
CT = DH // P
GRP, GC, GN = 32, 16, 64
GP = GRP // 2
L = 8
CK = SEQ // L
CS = CK + NB
NM = 256
MT = NM // P
XH, XD = 4, 256
NG, NE, FF = 4, 32, 256
EPS = 1e-6
TWO_PI = 2.0 * math.pi
PI_HI, PI_MID = 6.28125, 1.9350051879882812e-03
PI_LO = TWO_PI - PI_HI - PI_MID
ROUND = 12582912.0

VECS = [("g_mix", 8), ("g_mem", 8), ("g_xa", 8), ("g_moe", 8), ("s5_b_glu", 4), ("s5_d", 4),
        ("lru_conv_w", 16), ("lru_conv_b", 4), ("lru_b_a", 4), ("lru_b_x", 4), ("lru_lam", 4),
        ("state_lru_h", 32)]
COL, _at = {}, 0
for _n, _k in VECS:
    COL[_n] = _at
    _at += _k
NVEC = _at

SEMS = """x_in0 x_in1 x_in2 par_in lam_in bnat_in state_in gate_w_in win_in0 win_in1 wkv_in0 wkv_in1 wkv_in2 glu_in
u_out u_in y_out y_in klag_out t_in tp_full tp_free ta_full ta_free ma_full ma_free md_full md_free act_own
dve_own pool_own ident_ok std_ok xn_ok dt_ok ang_ok trig_ok scal_ok gnat_ok h_ok klag_ok wab_zero t_zero
small_ok par_ok spx_ok xc_ok te_ok sqrt_arg sq_ok ylru_ok end_ok hs_ok ydc_ok yg_ok lru_ends kv_out small_out
ut_in kv_in ys5_ok wout_in wq_in wo_in x_res0 x_res1 x_res2 sq2_ok xn2_ok xn2_st0 xn2_st1 mx_ok pn_ok smx_ok
spn_ok cache_in0 cache_in1 cache_in2 wr_in consts_ok lg_ok gexp_ok edif_ok eexp_ok a_ok r48_ok ro_ok ctl_ok
idx_ok ew_in0 ew_in1 ew_in2 ew_in3 xg_clear xg_in0 xg_in1 xg_in2 xg_in3 t_full t_free gu_full silu_ok prod_ok
ht_full htm_ok d_full ya_ok yd_done y_st0 y_st1 x_go xw_in xg_in xt_full xt_free xgu_full xsilu_ok xprod_ok
xht_full xhtm_ok xd_full xya_ok xyd_ok xy_st f_in0 f_in1 f_in2 gf_in f_sum f_std f_out f_st0 f_st1 f_st2
fin_x"""


def hybrid_layer(nc, I, O, W):
    f32, i32, u32 = mybir.dt.float32, mybir.dt.int32, mybir.dt.uint32
    ALU, ACT, AX = mybir.AluOpType, mybir.ActivationFunctionType, mybir.AxisListType
    MUL, ADD, SUB = ALU.mult, ALU.add, ALU.subtract
    ctx = ExitStack()
    with ctx:
        def sb(name, shape, dt=f32):
            return ctx.enter_context(nc.sbuf_tensor(name, shape, dt))

        sem = {n: ctx.enter_context(nc.semaphore(n)) for n in SEMS.split()}
        bank = [ctx.enter_context(nc.psum_tensor(f"bank{b}", [P, 512], f32)) for b in range(8)]

        ident = sb("ident", [P, P])
        par = sb("par", [P, 232])
        convst = par[:, 136:232].rearrange("p (s k c) -> p s k c", s=NB, k=3)
        rstd = sb("rstd", [P, 12])
        ssq = sb("ssq", [P, 12])
        m4sp, m8sp, spt = sb("m4sp", [P, 4]), sb("m8sp", [P, 4]), sb("spt", [P, 24])
        zero1 = sb("zero1", [P, 2])
        sp7 = sb("sp7", [P, 7, GP])
        pw = sb("pw", [P, 2, L + 1, GP])
        h0t = sb("h0t", [P, 2, NB, GP])
        fin = sb("fin", [P, 2, NB, GP])
        finp = sb("finp", [P, 2, GP])
        lh = sb("lh", [P, 1 + NB, CT])
        lc = sb("lc", [P, 1 + NB, 3, CT])
        rank_a = sb("arena", [P, 50960])

        def reg(at, *shape):
            n = 1
            for s in shape:
                n *= s
            ap = rank_a[:, at:at + n]
            if len(shape) == 1:
                return ap
            names = "abcdef"[:len(shape)]
            return ap.rearrange(f"p ({' '.join(names)}) -> p {' '.join(names)}", **dict(zip(names, shape)))

        R_KT, R_V, R_HT, R_UT, R_GL, R_XL = 0, 2048, 4096, 12800, 17152, 21504
        R_H, R_G, R_WR, R_TMP = 25964, 30572, 34668, 42860
        kt, vv = reg(R_KT, KD, NM), reg(R_V, MT, D)
        ht = reg(R_HT, KD, TOK)
        ut, gl = reg(R_UT, CT, TOK), reg(R_GL, CT, TOK)
        XLW = 3 + SEQ + NB * (3 + DS)
        xl = reg(R_XL, CT, XLW)
        hmat = reg(R_H, 2, GP, L + 1, GC)
        gmat = reg(R_G, GP, 2, P)
        tmat = reg(R_G, GRP, P)
        wkv = [reg(R_XL + 4096 * s, KD, 512) for s in range(3)]
        mt_ = reg(R_GL, KD, NM)
        kst = reg(R_GL + 2048, MT, D)
        win = [reg(R_WR + 4096 * s, KD, 512) for s in range(2)]
        xst = [reg(R_TMP + 1024 * s, D) for s in range(3)]
        q16 = reg(R_TMP + 3072, 20, P)
        bnat = reg(R_TMP + 5632, 2, GP, GC)
        bbar = reg(R_TMP + 6144, 2, GP, GC)
        craw = reg(R_TMP + 6656, 2, 4, P)
        cnat = reg(R_G, 2, GP, GC)
        ptmp = reg(R_TMP + 7680, 288)
        GH = 8
        gnat = reg(R_GL, 2, GH, L, GC)
        gtmp = reg(R_GL + 2048, GH, L, GC)
        htmp = reg(R_GL + 2048, GH, L + 1, GC)
        klag = reg(R_GL, GP, 2, P)
        uch = reg(R_WR + 4096, GRP, CS)
        xc = reg(R_TMP + 300, CT, TOK)
        lru_w = [[reg(a + 1088 * s, TOK) for s in range(3)] for a in (R_TMP + 300 + 4352, R_KT)]
        cost, sint = reg(R_KT, GP, CK), reg(R_V, GP, CK)
        st = reg(R_XL, 2, GP, CS)
        wglu = reg(R_WR, CT, DH)
        rot1, rot2 = reg(R_UT + 1024, GH, CK), reg(R_UT + 2048, GH, CK)
        yd = reg(R_XL, CT, TOK)
        sig = [reg(R_WR + 2560 + 408 * s, 408) for s in range(2)]
        wab = reg(R_UT, 2, CT, P)
        parin = q16[:, 0, :]
        cstin = q16[:, 1, :]

        class Count:
            def __init__(self):
                self.n = -1

            def next(self):
                self.n += 1
                return self.n

        TP, TA, MA, MD = (0, 1), (6, 7), (2, 3), (4, 5)
        stin = [q16[:, 0, :], q16[:, 1, :]]
        xl_t = reg(R_HT + 8448, 2 * P)
        s5_t = reg(R_WR + 2048, 4, P)
        TSPLIT = [(0, 3), (3, 6), (6, 8)]
        squares = reg(R_UT, D)
        ptmp2 = sb('ptmp2', [P, 96])
        st_flat = reg(R_XL, 2 * GP * CS)
        rot = [rot1, rot2]

        def tile_fills(n):
            return 1 + 2 * (n + 1) + (4 if n >= 5 else 0)

        HT_READY = [tile_fills(5), tile_fills(9), tile_fills(10)]
        G_TP0 = tile_fills(10) + 4
        MA_Q = 8 + 36 + 24 + 16 + 12 + 24
        MA_PV = MA_Q
        MA_R = MA_PV + 16 + NB + NT
        TP_XA = G_TP0 + 8 + 2
        TP_P = TP_XA + 2 * NT
        TP_M = TP_P + 16 + 5 * NB
        Y_TA0 = 8

        R_E2 = R_XL + NT * D
        xres = reg(R_XL, NT, D)
        wout = reg(R_HT, KD, D)
        h2 = reg(50960 - KD * TOK, KD, TOK)
        wq = reg(R_E2, KD, D)
        wo = reg(R_UT, KD, D)
        qq = ht
        xns = [reg(R_E2 + 8192 + D * s, D) for s in range(2)]
        squares2, squares3 = reg(R_E2 + 8192 + 2320, D), reg(R_E2 + 6144, D)
        cache = [reg(a, 2, MT, D) for a in (R_UT, R_UT + 4096, R_E2 + 4096)]
        CSLOT = [0, 1, 2, 0, 1, 2, 0, 2]
        PV_DONE = [MA_PV + 3 * b + 5 for b in range(7)] + [MA_PV + 16 + NB]
        prob = [reg(R_E2 + 8192 + 1024 * s, 4, NM) for s in range(2)]
        ptr = reg(R_E2 + 8192 + 2048, MT, 512)
        ktb = reg(R_E2, KD, NM)
        probs = [reg(R_E2 + 2048 + NM * s, NM) for s in range(2)]
        pts = reg(R_E2 + 2560, MT, P)
        smx, srs = sb("smx", [P, 16]), sb("srs", [P, 16])
        wr = sb("wr", [P, KD, NG + NE])
        wcomb = sb("wcomb", [P, NT, 2])
        idxg, idxs = sb("idxg", [P, 48], u32), sb("idxs", [P, 48], u32)
        gcol = sb("gcol", [P, 2], u32)
        ctl = sb("ctl", [1, 20], i32)
        ones, tri, iota = (reg(R_UT + KD * D + P * j, P) for j in range(3))
        val = reg(R_UT + KD * D + 3 * P, NT, 2)
        lg = reg(R_E2 + 8192 + 2048, NT, NG + NE)
        R_M = 50960 - KD * TOK
        xgt = [reg(R_M + 1024 * s, KD, P) for s in range(2)]
        hsil = [reg(R_M + 2048 + FF * s, FF) for s in range(2)]
        hpr = [reg(R_M + 2560 + FF * s, FF) for s in range(2)]
        htr = [reg(R_M + 3072 + FF * s, 2, P) for s in range(2)]
        yst = [reg(R_M + 3584 + D * s, D) for s in range(2)]
        R_R = R_M + 5632
        le, oh = reg(R_R, NT, NE), reg(R_R + 288, NT, 2, NE)
        r48 = reg(R_R, NT, 2, 48)
        aa, ac, otmp = reg(R_R + 864, NT, NE), reg(R_R + 1152, NT, NE), reg(R_R + 1440, NT, 2, NE)
        m8, i8f, g8 = reg(R_R + 2016, NT, 8), reg(R_R + 2088, NT, 8), reg(R_R + 2160, NT, 8)
        i8 = i8f.bitcast(u32)
        sm = reg(R_R + 2232, 16, 2 * NT)
        cnt = reg(R_R + 2520, 4, NE)
        ovf = reg(R_R + 2648, 20)
        ovt = reg(R_E2 + 8192, 16, NE)
        ro = [reg(R_E2 + 8192 + 256 * s, 2, P) for s in range(8)]
        ew = [reg(a, 6144) for a in (0, 6144, R_E2, R_UT)]
        xg = [reg(R_E2 + 6144 + D * s, D) for s in range(2)] + [reg(R_UT + 6144 + D * s, D) for s in range(2)]
        fy = [reg(2048 * s, 2, D) for s in range(3)]
        fo = [reg(6144 + D * s, D) for s in range(3)]
        gfin, squaresf = reg(9216, D), reg(10240, D)
        SLOTS = NE + 16
        cm = lambda j: sm[:, j, :]
        block = ctx.enter_context(nc.Block())

        @block.sync
        def _(sp):
            for name, rows in VECS:
                sp.dma_start(parin[COL[name]:COL[name] + rows, :], I[name]).then_inc(sem["par_in"], 16)
            sp.dma_start(cstin[0:NB * 3 * CT, :], I["state_lru_conv"]).then_inc(sem["par_in"], 16)

            def load_x(n):
                if n >= 3:
                    sp.wait_ge(sem["tp_full"], tile_fills(n - 3))
                src = I["mem"][n * P:(n + 1) * P, :] if n < MT else I["x"][(n - MT) * P:(n - MT) * P + ROWS[n - MT], :]
                sp.dma_start(xst[n % 3][0:src.shape[0], :], src).then_inc(sem[f"x_in{n % 3}"], 16)

            for n in range(3):
                load_x(n)
            for q, (w, half) in enumerate([("wk", 0), ("wk", 1), ("wv", 0)]):
                sp.dma_start(wkv[q][:, :, :], I[w][:, half * 512:half * 512 + 512].rearrange("(k p) n -> p k n", p=P)).then_inc(sem[f"wkv_in{q}"], 16)
            load_x(3)
            load_x(4)
            for src, dst in ((I["lam_re"], q16[0:GP, 2, :]), (I["lam_im"], q16[0:GP, 3, :]), (I["log_dt"], ptmp[0:GP, 256:258])):
                sp.dma_start(dst, src).then_inc(sem["lam_in"], 16)
            for ri in range(2):
                sp.dma_start(bnat[:, ri, :, :], I["b"][ri]).then_inc(sem["bnat_in"], 16)
                for j in range(4):
                    for l in range(2):
                        sp.dma_start(craw[:, ri, j, 64 * l:64 * l + 64], I["c"][ri][j * P:j * P + P, :]).then_inc(sem["bnat_in"], 16)
            for s, c0 in ((0, DH), (1, 0)):
                sp.dma_start(win[s][:, :, :], I["w_in"][:, c0:c0 + 512].rearrange("(k p) n -> p k n", p=P)).then_inc(sem[f"win_in{s}"], 16)
            sp.wait_ge(sem["ma_full"], 2)
            sp.dma_start(wkv[0][:, :, :], I["wv"][:, 512:1024].rearrange("(k p) n -> p k n", p=P)).then_inc(sem["wkv_in0"], 16)
            for n in range(5, NT + MT):
                load_x(n)
            sp.wait_ge(sem["ma_free"], 8)
            sp.dma_start(O["mem_k"].rearrange("(m p) d -> p m d", p=P), kst[:, :, :]).then_inc(sem["kv_out"], 16)
            sp.dma_start(O["mem_v"].rearrange("(m p) d -> p m d", p=P), vv[:, :, :]).then_inc(sem["kv_out"], 16)
            sp.wait_ge(sem["tp_free"], tile_fills(4) + 4)
            sp.dma_start(W["kt"], kt[:, :, :].rearrange("p k m -> p (k m)")).then_inc(sem["kv_out"], 16)
            sp.wait_ge(sem["ma_full"], 20)
            sp.dma_start(win[0][:, :, :], I["w_in"][:, 1024:1536].rearrange("(k p) n -> p k n", p=P)).then_inc(sem["win_in0"], 16)
            sp.wait_ge(sem["ma_free"], 8 + 24)
            sp.dma_start(W["u"].rearrange("(k p) t -> p k t", p=P), ut[:, :, :]).then_inc(sem["u_out"], 16)
            sp.wait_ge(sem["u_out"], 16)
            sp.wait_ge(sem["ma_full"], 32)
            for t in range(L):
                sp.dma_start(uch[16 * (L - 1 - t):16 * (L - t), :, :], W["u"].rearrange("(g c) (t k) -> t c g k", c=GC, t=L)[t]).then_inc(sem["u_in"], 16)
            sp.wait_ge(sem["wab_zero"], 1)
            for a, w in enumerate(("w_a", "w_x")):
                for h in range(2):
                    sp.dma_start(wab[64 * h:64 * h + 64, a, :, 64 * h:64 * h + 64], I[w][h]).then_inc(sem["gate_w_in"], 16)
            sp.wait_ge(sem["t_zero"], 1)
            sp.wait_ge(sem["klag_out"], 16)
            for s in range(L):
                sp.dma_start(tmat[16 * (L - 1 - s):16 * (L - s), :, 16 * s:P],
                             W["klag"].rearrange("c (g n) -> c g n", g=GRP)[:, :, 0:P - 16 * s]).then_inc(sem["t_in"], 16)
            sp.wait_ge(sem["ma_full"], 60)
            sp.dma_start(wglu[:, :, :], I["w_glu"].rearrange("(k p) n -> p k n", p=P)).then_inc(sem["glu_in"], 16)
            sp.wait_ge(sem["ta_free"], Y_TA0 + GRP)
            for t in range(L):
                sp.dma_start(W["y"].rearrange("(g c) (t k) -> t c g k", c=GC, t=L)[t], uch[16 * t:16 * t + 16, :, :]).then_inc(sem["y_out"], 16)
            sp.wait_ge(sem["y_out"], 16 * L)
            sp.dma_start(yd[:, :, :], W["y"].rearrange("(k p) t -> p k t", p=P)).then_inc(sem["y_in"], 16)
            sp.wait_ge(sem["ma_full"], 84)
            sp.wait_ge(sem["end_ok"], 1)
            sp.dma_start(ut[:, :, :], W["u"].rearrange("(k p) t -> p k t", p=P)).then_inc(sem["ut_in"], 16)
            sp.wait_ge(sem["small_ok"], 2)
            ends = xl_t
            sp.dma_start(O["lru_h_p"], ends[0:4, 0:P]).then_inc(sem["small_out"], 16)
            sp.dma_start(O["lru_h_s"], ends[4:36, 0:P]).then_inc(sem["small_out"], 16)
            sp.dma_start(O["lru_c_p"], ends[0:12, P:2 * P]).then_inc(sem["small_out"], 16)
            sp.dma_start(O["lru_c_s"], ends[12:108, P:2 * P]).then_inc(sem["small_out"], 16)
            sp.wait_ge(sem["small_ok"], 3)
            for ri in range(2):
                sp.dma_start(O["s5_s"][ri], s5_t[:, ri, :]).then_inc(sem["small_out"], 16)
                sp.dma_start(O["s5_p"][ri], s5_t[0:GP, 2 + ri, :]).then_inc(sem["small_out"], 16)
            sp.wait_ge(sem["ylru_ok"], CT)
            sp.dma_start(kt[:, :, :].rearrange("p k m -> p (k m)"), W["kt"]).then_inc(sem["kv_in"], 16)
            sp.dma_start(vv[:, :, :], O["mem_v"].rearrange("(m p) d -> p m d", p=P)).then_inc(sem["kv_in"], 16)

            sp.wait_ge(sem["ta_full"], Y_TA0 + GRP)
            sp.dma_start(wout[:, :, :], I["w_out"].rearrange("(k p) n -> p k n", p=P)).then_inc(sem["wout_in"], 16)
            sp.wait_ge(sem["ys5_ok"], 3 * CT)
            for g in range(2):
                sp.dma_start(xres[:, 4 * g:4 * g + 4, :], I["x"][512 * g:512 * g + 512, :].rearrange("(i p) d -> p i d", p=P)).then_inc(sem[f"x_res{g}"], 16)
            sp.dma_start(xres[0:ROWS[8], 8, :], I["x"][SEQ:TOK, :]).then_inc(sem["x_res2"], 16)
            sp.wait_ge(sem["small_out"], 128)
            sp.dma_start(wq[:, :, :], I["w_q"].rearrange("(k p) n -> p k n", p=P)).then_inc(sem["wq_in"], 16)
            sp.dma_start(wr[:, :, 0:NG], I["w_group"].rearrange("(k p) n -> p k n", p=P)).then_inc(sem["wr_in"], 16)
            sp.dma_start(wr[:, :, NG:], I["w_expert"].rearrange("(k p) n -> p k n", p=P)).then_inc(sem["wr_in"], 16)
            sp.wait_ge(sem["md_full"], 2 * NT)
            for b in range(NB):
                slot = CSLOT[b]
                if b == 2:
                    sp.wait_ge(sem["ma_full"], MA_Q)
                if slot in CSLOT[:b]:
                    sp.wait_ge(sem["ma_full"], PV_DONE[max(o for o in range(b) if CSLOT[o] == slot)])
                for j, w in enumerate(("ck", "cv")):
                    sp.dma_start(cache[slot][:, j, :, :], I[w][b * NM:b * NM + NM, :].rearrange("(m p) d -> p m d", p=P)).then_inc(sem[f"cache_in{slot}"], 16)
                for after, k0 in ((6, 4), (7, 0)):
                    if b == after:
                        sp.wait_ge(sem["ma_full"], PV_DONE[(4, 6)[after - 6]])
                        sp.dma_start(wo[:, k0:k0 + 4, :], I["w_o"][k0 * P:k0 * P + 512, :].rearrange("(k p) n -> p k n", p=P)).then_inc(sem["wo_in"], 16)

            def load_expert(e, buf, s="ew_in"):
                gu = buf[:, 0:4096].rearrange("p (k n) -> p k n", k=KD)
                dn = buf[:, 4096:6144].rearrange("p (k n) -> p k n", k=2)
                for src, dst in ((I["w_gate"], gu[:, :, 0:FF]), (I["w_up"], gu[:, :, FF:]), (I["w_down"], dn)):
                    if isinstance(e, int):
                        v = src[e].rearrange("(k p) n -> p k n", p=P)
                    else:
                        v = src[bass.ds(e, 1)].rearrange("e (k p) n -> p (e k) n", p=P)
                    sp.dma_start(dst, v).then_inc(s, 16)

            sp.wait_ge(sem["ma_full"], MA_PV + 16 + NB)
            sp.wait_ge(sem["ma_free"], MA_PV + 16 + NB)
            for e in range(3):
                load_expert(e, ew[e], sem[f"ew_in{e}"])
            for i in range(NT):
                sp.wait_ge(sem["xn2_ok"], NT + i + 1)
                sp.dma_start(W["xn"][i * P:i * P + ROWS[i], :], xns[i % 2][0:ROWS[i], :]).then_inc(sem[f"xn2_st{i % 2}"], 16)
            sp.wait_ge(sem["md_full"], 4 * NT)
            load_expert(3, ew[3], sem["ew_in3"])
            with sp.Fori(1, NE // 4) as i:
                for b in range(4):
                    sp.wait_ge(sem["d_full"], i * 4 + (b - 3))
                    load_expert(i * 4 + b, ew[b], sem[f"ew_in{b}"])
            sp.wait_ge(sem["ctl_ok"], 1)
            with sp.If(sp.value_load(ctl[0:1, 16:17], min_val=0, max_val=16) > 0):
                with sp.Fori(0, 16) as i:
                    sp.wait_ge(sem["x_go"], i + 1)
                    ev = sp.value_load(ctl[0:1, bass.ds(i, 1)], min_val=0, max_val=NE - 1)
                    load_expert(ev, ew[0], sem["xw_in"])
            sp.wait_ge(sem["d_full"], NE - 2)
            sp.wait_ge(sem["ew_in1"], 48 * NE // 4)
            sp.dma_start(gfin[:, :], I["g_final"].to_broadcast([P, D])).then_inc(sem["gf_in"], 16)
            sp.wait_ge(sem["fin_x"], 1)
            for i in range(NT + 2):
                if i < NT:
                    r = ROWS[i]
                    if i >= 3:
                        sp.wait_ge(sem["f_sum"], i - 2)
                    for c in range(2):
                        sp.dma_start(fy[i % 3][0:r, c, :], W["moe"][c * TOK + i * P:c * TOK + i * P + r, :]).then_inc(sem[f"f_in{i % 3}"], 16)
                if i >= 2:
                    o = i - 2
                    sp.wait_ge(sem["f_out"], o + 1)
                    dst = O["y_p"][o * P:o * P + P, :] if o < 8 else O["y_s"]
                    sp.dma_start(dst, fo[o % 3][0:ROWS[o], :]).then_inc(sem[f"f_st{o % 3}"], 16)
            for o in range(3):
                sp.wait_ge(sem[f"f_st{o}"], 48)
            sp.wait_ge(sem["kv_out"], 48)

        @block.gpsimd
        def _(pool):
            nc.gpsimd.memset(ident[:, :], 0.0).then_inc(sem["pool_own"], 1)
            pool.wait_ge(sem["pool_own"], 1)
            nc.gpsimd.affine_select(out=ident[:, :], in_=ident[:, :], compare_op=ALU.not_equal, fill=1.0, base=0,
                                    pattern=[[-1, P]], channel_multiplier=1).then_inc(sem["pool_own"], 1)
            nc.gpsimd.memset(zero1[:, 0:1], 0.0).then_inc(sem["pool_own"], 1)
            nc.gpsimd.memset(zero1[:, 1:2], EPS).then_inc(sem["pool_own"], 1)
            pool.wait_ge(sem["pool_own"], 4)
            nc.gpsimd.memset(par[:, 104:136], 0.0).then_inc(sem["ident_ok"], 1)
            pool.wait_ge(sem["par_ok"], 1)
            for ri in range(2):
                pool.dma_start(stin[ri], I["state_s5"][ri]).then_inc(sem["state_in"], 16)
            pool.wait_ge(sem["klag_ok"], 8)
            pool.dma_start(W["klag"].rearrange("c (g n) -> c g n", g=GRP), klag[0:16, :, :, :].rearrange("c a b n -> c (a b) n")).then_inc(sem["klag_out"], 16)
            pool.wait_ge(sem["u_out"], 16)
            nc.gpsimd.memset(wab[:, :, :, :], 0.0).then_inc(sem["wab_zero"], 1)
            pool.wait_ge(sem["ma_full"], 52)
            nc.gpsimd.memset(tmat[:, :, :], 0.0).then_inc(sem["t_zero"], 1)

            pool.wait_ge(sem["md_full"], 2 * NT)
            nc.gpsimd.memset(ones[:, :], 1.0).then_inc(sem["pool_own"], 1)
            nc.gpsimd.memset(tri[:, :], 1.0).then_inc(sem["pool_own"], 1)
            nc.gpsimd.iota(iota[:, :], pattern=[[1, P]], base=0, channel_multiplier=0, allow_small_or_imprecise_dtypes=True).then_inc(sem["pool_own"], 1)
            nc.gpsimd.iota(val[:, :, :], pattern=[[P, NT], [TOK, 2]], base=1, channel_multiplier=1, allow_small_or_imprecise_dtypes=True).then_inc(sem["pool_own"], 1)
            pool.wait_ge(sem["pool_own"], 8)
            nc.gpsimd.affine_select(out=tri[:, :], in_=tri[:, :], compare_op=ALU.is_gt, fill=0.0, base=0, pattern=[[1, P]],
                                    channel_multiplier=-1).then_inc(sem["pool_own"], 1)
            pool.wait_ge(sem["pool_own"], 9)
            nc.gpsimd.memset(val[ROWS[8]:P, NT - 1, :], 0.0).then_inc(sem["pool_own"], 1)
            pool.wait_ge(sem["pool_own"], 10)
            pool.wait_ge(sem["ma_full"], MA_PV + 16 + NB)
            nc.gpsimd.memset(lg[:, :, :], 0.0).then_inc(sem["consts_ok"], 1)
            pool.wait_ge(sem["sq2_ok"], 2 * NT)
            pool.wait_ge(sem["md_full"], 4 * NT)
            for b in range(4):
                nc.gpsimd.memset(xg[b][:, :], 0.0).then_inc(sem["xg_clear"], 1)
            pool.wait_ge(sem["xg_clear"], 4)
            pool.wait_ge(sem["idx_ok"], 1)
            pool.wait_ge(sem["xn2_st0"], 80)
            pool.wait_ge(sem["xn2_st1"], 64)

            def fetch(slot, b, done):
                nc.gpsimd.indirect_dma_start(out=xg[b][:, :], out_offset=None, in_=W["xn"],
                                             in_offset=bass.IndirectOffsetOnAxis(ap=idxg[:, slot:slot + 1], axis=0),
                                             bounds_check=TOK - 1, oob_is_err=False).then_inc(sem[done], 16)

            def store(slot, b, done):
                nc.gpsimd.indirect_dma_start(out=W["moe"], out_offset=bass.IndirectOffsetOnAxis(ap=idxs[:, slot:slot + 1], axis=0),
                                             in_=yst[b % 2][:, :], in_offset=None,
                                             bounds_check=2 * TOK - 1, oob_is_err=False).then_inc(sem[done], 16)

            for e in range(4):
                fetch(e, e, f"xg_in{e}")
            for e in range(NE):
                if e + 4 < NE:
                    pool.wait_ge(sem["t_full"], e * 2 + 2)
                    pool.wait_ge(sem[f"xg_in{e % 4}"], (e // 4 + 1) * 16)
                    fetch(e + 4, e % 4, f"xg_in{e % 4}")
                pool.wait_ge(sem["ya_ok"], e + 1)
                pool.wait_ge(sem["yd_done"], e + 1)
                if e >= 2:
                    pool.wait_ge(sem[f"y_st{e % 2}"], (e // 2) * 16)
                store(e, e, f"y_st{e % 2}")
            for b in range(2):
                pool.wait_ge(sem[f"y_st{b}"], 16 * NE // 2)
            pool.wait_ge(sem["ctl_ok"], 1)
            with pool.If(pool.value_load(ctl[0:1, 16:17], min_val=0, max_val=16) > 0):
                for x in range(16):
                    nc.gpsimd.tensor_copy(gcol[:, 0:1], idxg[:, 0:1]).then_inc(sem["x_go"], 1)
                    pool.wait_ge(sem["x_go"], x + 1)
                    fetch(NE + x, 0, "xg_in")
                    pool.wait_ge(sem["xya_ok"], x + 1)
                    pool.wait_ge(sem["xyd_ok"], x + 1)
                    store(NE + x, 0, "xy_st")
                    pool.wait_ge(sem["xy_st"], (x + 1) * 16)
            nc.gpsimd.tensor_copy(gcol[:, 1:2], idxg[:, 0:1]).then_inc(sem["fin_x"], 1)

        @block.tensor
        def _(pe):
            tp, ta, ma, md = Count(), Count(), Count(), Count()

            def claim(ring, count, free):
                n = count.next()
                if n >= 2:
                    pe.wait_ge(sem[free], n - 1)
                return bank[ring[n % 2]]

            pe.wait_ge(sem["ident_ok"], 1)
            pe.wait_ge(sem["par_in"], 16 * (len(VECS) + 1))
            b = claim(TP, tp, "tp_free")
            nc.tensor.transpose(b[:, 0:NVEC], parin[0:NVEC, :], ident[0:NVEC, 0:NVEC])
            nc.tensor.transpose(b[:, 136:232], cstin[0:96, :], ident[0:96, 0:96]).then_inc(sem["tp_full"], 1)

            def norm_t(n):
                r = P if n < MT else ROWS[n - MT]
                pe.wait_ge(sem["xn_ok"], n + 1)
                for hf in range(2):
                    b = claim(TP, tp, "tp_free")
                    for k in range(4):
                        c = (hf * 4 + k) * P
                        last = nc.tensor.transpose(b[:, k * P:k * P + r], xst[n % 3][0:r, c:c + P], ident[0:r, 0:r])
                    last.then_inc(sem["tp_full"], 1)

            def memory(q):
                pe.wait_ge(sem[f"wkv_in{q % 3}"], 16 * (q // 3 + 1))
                for m in range(MT):
                    b = claim(MA, ma, "ma_free")
                    for k in range(KD):
                        last = nc.tensor.matmul(b[:, :], mt_[:, k, m * P:m * P + P], wkv[q % 3][:, k, :], start=k == 0, stop=k == KD - 1)
                    last.then_inc(sem["ma_full"], 1)

            for n in range(3):
                norm_t(n)
            pe.wait_ge(sem["tp_free"], 5)
            memory(0)
            norm_t(3)
            norm_t(4)
            memory(1)
            for m in range(MT):
                pe.wait_ge(sem["ma_free"], 4)
                for hf in range(2):
                    b = claim(TP, tp, "tp_free")
                    for k in range(4):
                        c = (hf * 4 + k) * P
                        last = nc.tensor.transpose(b[:, k * P:k * P + P], kst[:, m, c:c + P], ident[:, :])
                    last.then_inc(sem["tp_full"], 1)
            for n in range(5, 8):
                norm_t(n)
            memory(2)
            memory(3)
            for n in range(8, NT + MT):
                norm_t(n)

            def project(g, slot, fills, chunks=range(3)):
                pe.wait_ge(sem[f"win_in{slot}"], fills * 16)
                for ci in chunks:
                    c0, w = CHUNKS[ci]
                    if g == 0:
                        pe.wait_ge(sem["tp_free"], HT_READY[ci])
                    for m in range(CT):
                        b = claim(MA, ma, "ma_free")
                        for k in range(KD):
                            last = nc.tensor.matmul(b[:, 0:w], win[slot][:, k, m * P:m * P + P], ht[:, k, c0:c0 + w], start=k == 0, stop=k == KD - 1)
                        last.then_inc(sem["ma_full"], 1)

            project(0, 0, 1, [0])
            pe.wait_ge(sem["scal_ok"], 1)
            b = claim(TP, tp, "tp_free")
            for j in range(7):
                last = nc.tensor.transpose(b[:, j * GP:j * GP + GP], q16[0:GP, 11 + j, :], ident[0:GP, 0:GP])
            last.then_inc(sem["tp_full"], 1)
            pe.wait_ge(sem["bnat_in"], 16 * 18)
            for ri in range(2):
                b = claim(TP, tp, "tp_free")
                for j in range(4):
                    last = nc.tensor.transpose(b[:, j * P:j * P + P], craw[:, ri, j, :], ident[:, :])
                last.then_inc(sem["tp_full"], 1)
            pe.wait_ge(sem["state_in"], 32)
            b = claim(TP, tp, "tp_free")
            for ri in range(2):
                last = nc.tensor.transpose(b[:, ri * P:ri * P + P], stin[ri], ident[:, :])
            last.then_inc(sem["tp_full"], 1)
            project(0, 0, 1, [1, 2])
            project(1, 1, 1, [0, 1])
            for h in range(GP // GH):
                pe.wait_ge(sem["gnat_ok"], h + 1)
                for q in range(GH * 2 // 4):
                    b = claim(TP, tp, "tp_free")
                    for j in range(4):
                        gp, ri = (q * 4 + j) // 2, (q * 4 + j) % 2
                        last = nc.tensor.transpose(b[:, j * P:j * P + P], gnat[:, ri, gp, :, :].rearrange("p t c -> p (t c)"), ident[:, :])
                    last.then_inc(sem["tp_full"], 1)
                if h == 0:
                    project(1, 1, 1, [2])
            pe.wait_ge(sem["h_ok"], 1)
            for q in range(4):
                for l in range(2):
                    b = claim(TA, ta, "ta_free")
                    for j in range(4):
                        gp = q * 4 + j
                        for ri in range(2):
                            last = nc.tensor.matmul(b[0:GC, j * P:j * P + P], bbar[64 * l:64 * l + 64, ri, gp, :],
                                                    hmat[64 * l:64 * l + 64, ri, gp, 0:L, :].rearrange("p t c -> p (t c)"), start=ri == 0, stop=ri == 1)
                    last.then_inc(sem["ta_full"], 1)
            project(2, 0, 2, [0])
            pe.wait_ge(sem["u_in"], 16 * L)
            pe.wait_ge(sem["tp_free"], G_TP0 + 8)
            for gp in range(GP):
                b = claim(MA, ma, "ma_free")
                for ri in range(2):
                    for l in range(2):
                        last = nc.tensor.matmul(b[64 * l:64 * l + 64, ri * CS:ri * CS + CS], gmat[:, gp, ri, 64 * l:64 * l + 64],
                                                uch[:, 2 * gp + l, :], start=True, stop=True)
                last.then_inc(sem["ma_full"], 1)
            project(2, 0, 2, [1, 2])

            def gates(c):
                if c == 0:
                    pe.wait_ge(sem["gate_w_in"], 64)
                    pe.wait_ge(sem["xc_ok"], CT)
                for a in range(2):
                    for c0, w in CHUNKS:
                        b = claim(MA, ma, "ma_free")
                        nc.tensor.matmul(b[:, 0:w], wab[:, a, c, :], xc[:, c, c0:c0 + w], start=True, stop=True).then_inc(sem["ma_full"], 1)

            gates(0)
            pe.wait_ge(sem["hs_ok"], 1)
            pe.wait_ge(sem["t_in"], 16 * L)
            for gp in range(GP):
                if gp in (8, 12):
                    gates(gp // 4 - 1)
                for l in range(2):
                    b = claim(TA, ta, "ta_free")
                    g, o = 2 * gp + l, 0
                    nc.tensor.matmul(b[:, o:o + CS], tmat[:, g, :], uch[:, g, :], start=True, stop=False)
                    for ri in range(2):
                        last = nc.tensor.matmul(b[:, o + 1:o + CS], hmat[64 * l:64 * l + 64, ri, gp, 1:L + 1, :].rearrange("p t c -> p (t c)"),
                                                st[64 * l:64 * l + 64, ri, gp, 0:CS - 1], start=False, stop=ri == 1)
                    last.then_inc(sem["ta_full"], 1)
            gates(3)
            pe.wait_ge(sem["lru_ends"], 1)
            b = claim(TP, tp, "tp_free")
            nc.tensor.transpose(b[0:36, 0:P], lh[:, :, :].rearrange("p s c -> p (s c)"), ident[:, :])
            nc.tensor.transpose(b[0:108, P:2 * P], lc[:, :, :, :].rearrange("p s k c -> p (s k c)"), ident[:, :]).then_inc(sem["tp_full"], 1)
            pe.wait_ge(sem["end_ok"], 1)
            b = claim(TP, tp, "tp_free")
            for ri in range(2):
                nc.tensor.transpose(b[:, ri * P:ri * P + P], fin[:, ri, :, :].rearrange("p s g -> p (s g)"), ident[:, :])
            for ri in range(2):
                last = nc.tensor.transpose(b[0:GP, (2 + ri) * P:(3 + ri) * P], finp[:, ri, :], ident[:, :])
            last.then_inc(sem["tp_full"], 1)
            pe.wait_ge(sem["glu_in"], 16)
            for c in range(CT):
                pe.wait_ge(sem["yg_ok"], c + 1)
            for t0, t1 in TSPLIT:
                for m in range(CT):
                    b = claim(MA, ma, "ma_free")
                    for k in range(CT):
                        last = nc.tensor.matmul(b[:, 0:(t1 - t0) * CS], wglu[:, k, m * P:m * P + P], yd[:, k, t0 * CS:t1 * CS], start=k == 0, stop=k == CT - 1)
                    last.then_inc(sem["ma_full"], 1)

            def resid(i, lhs, w):
                if i == 0:
                    pe.wait_ge(sem[w[1]], w[2])
                for nh in range(2):
                    b = claim(MD, md, "md_free")
                    for k in range(KD):
                        last = nc.tensor.matmul(b[0:ROWS[i], :], lhs(k, i), w[0][:, k, nh * 512:nh * 512 + 512], start=k == 0, stop=k == KD - 1)
                    last.then_inc(sem["md_full"], 1)

            def norm2_t(i, done):
                pe.wait_ge(sem["xn2_ok"], done + i + 1)
                r = ROWS[i]
                for hf in range(2):
                    b = claim(TP, tp, "tp_free")
                    for k in range(4):
                        c = (hf * 4 + k) * P
                        last = nc.tensor.transpose(b[:, k * P:k * P + r], xns[i % 2][0:r, c:c + P], ident[0:r, 0:r])
                    last.then_inc(sem["tp_full"], 1)

            def query(ci):
                c0, w = CHUNKS[ci]
                for m in range(KD):
                    b = claim(MA, ma, "ma_free")
                    for k in range(KD):
                        last = nc.tensor.matmul(b[:, 0:w], wq[:, k, m * P:m * P + P], h2[:, k, c0:c0 + w], start=k == 0, stop=k == KD - 1)
                    last.then_inc(sem["ma_full"], 1)

            pe.wait_ge(sem["ys5_ok"], 3 * CT)
            pe.wait_ge(sem["ylru_ok"], CT)
            for i in range(NT):
                resid(i, lambda k, i: (ut if k < CT else gl)[:, k % CT, i * P:i * P + ROWS[i]], (wout, "wout_in", 16))
                if i >= 1:
                    norm2_t(i - 1, 0)
            pe.wait_ge(sem["wq_in"], 16)
            pe.wait_ge(sem["tp_free"], TP_XA + 8)
            query(0)
            norm2_t(8, 0)
            pe.wait_ge(sem["tp_free"], TP_XA + 16)
            query(1)
            pe.wait_ge(sem["tp_free"], TP_XA + 18)
            query(2)

            def scores(s):
                c, h = s // XH, s % XH
                if s == 0:
                    pe.wait_ge(sem["ma_free"], MA_Q)
                for j in range(2):
                    b = claim(TA, ta, "ta_free")
                    for t in range(2):
                        c0 = c * 512 + (j * 2 + t) * P
                        for d in range(2):
                            last = nc.tensor.matmul(b[:, t * NM:t * NM + NM], qq[:, 2 * h + d, c0:c0 + P], kt[:, 2 * h + d, :], start=d == 0, stop=d == 1)
                    last.then_inc(sem["ta_full"], 1)

            pe.wait_ge(sem["kv_in"], 32)
            def cache_t(s):
                slot = CSLOT[s]
                pe.wait_ge(sem[f"cache_in{slot}"], 32 * (CSLOT[:s].count(slot) + 1))
                for m in range(MT):
                    for hf in range(2):
                        b = claim(TP, tp, "tp_free")
                        for k in range(4):
                            c = (hf * 4 + k) * P
                            last = nc.tensor.transpose(b[:, k * P:k * P + P], cache[slot][:, 0, m, c:c + P], ident[:, :])
                        last.then_inc(sem["tp_full"], 1)
                return tp.n + 1

            def sample_scores(s, ktb_n):
                pe.wait_ge(sem["tp_free"], ktb_n)
                b = claim(TA, ta, "ta_free")
                q0 = SEQ + 32 * (s // 4)
                for h in range(XH):
                    for d in range(2):
                        last = nc.tensor.matmul(b[32 * h:32 * h + 32, 0:NM], qq[:, 2 * h + d, q0:q0 + 32], ktb[:, 2 * h + d, :], start=d == 0, stop=d == 1)
                last.then_inc(sem["ta_full"], 1)

            def sample_pt(s):
                pe.wait_ge(sem["spn_ok"], s + 1)
                b = claim(TP, tp, "tp_free")
                for m in range(MT):
                    last = nc.tensor.transpose(b[:, m * P:m * P + P], probs[s % 2][:, m * P:m * P + P], ident[:, :])
                last.then_inc(sem["tp_full"], 1)
                return tp.n + 1

            def sample_pv(s, pts_n):
                pe.wait_ge(sem["tp_free"], pts_n)
                b = claim(MA, ma, "ma_free")
                for k in range(KD):
                    c0 = 32 * (k // 2) + DS * (s % 4)
                    for m in range(MT):
                        last = nc.tensor.matmul(b[:, k * DS:k * DS + DS], cache[CSLOT[s]][:, 1, m, k * P:k * P + P], pts[:, m, c0:c0 + DS], start=m == 0, stop=m == MT - 1)
                last.then_inc(sem["ma_full"], 1)

            scores(0)
            for s in range(8):
                for j in range(2):
                    pe.wait_ge(sem["pn_ok"], 2 * s + j + 1)
                    b = claim(TP, tp, "tp_free")
                    for t in range(2):
                        for m in range(MT):
                            last = nc.tensor.transpose(b[:, (t * 2 + m) * P:(t * 2 + m + 1) * P], prob[s % 2][:, 2 * j + t, m * P:m * P + P], ident[:, :])
                    last.then_inc(sem["tp_full"], 1)
                ptr_n = tp.n + 1
                ktb_n = cache_t(s)
                if s >= 1:
                    pts_n = sample_pt(s - 1)
                if s + 1 < 8:
                    scores(s + 1)
                pe.wait_ge(sem["tp_free"], ptr_n)
                h = s % XH
                for d in range(2):
                    b = claim(MA, ma, "ma_free")
                    for m in range(MT):
                        last = nc.tensor.matmul(b[:, :], vv[:, m, h * XD + d * P:h * XD + d * P + P], ptr[:, m, :], start=m == 0, stop=m == MT - 1)
                    last.then_inc(sem["ma_full"], 1)
                if s >= 1:
                    sample_pv(s - 1, pts_n)
                sample_scores(s, ktb_n)
            sample_pv(NB - 1, sample_pt(NB - 1))

            def router(i):
                if i == 0:
                    pe.wait_ge(sem["wr_in"], 32)
                pe.wait_ge(sem["tp_free"], TP_M + 2 * i + 2)
                b = claim(MA, ma, "ma_free")
                for k in range(KD):
                    last = nc.tensor.matmul(b[0:ROWS[i], 0:NG + NE], h2[:, k, i * P:i * P + ROWS[i]], wr[:, k, :], start=k == 0, stop=k == KD - 1)
                last.then_inc(sem["ma_full"], 1)

            pe.wait_ge(sem["ma_free"], MA_PV + 16 + NB)
            for i in range(NT):
                resid(i, lambda k, i: h2[:, k, i * P:i * P + ROWS[i]], (wo, "wo_in", 32))
                if i >= 1:
                    norm2_t(i - 1, NT)
                if i >= 2:
                    router(i - 2)
            norm2_t(8, NT)
            router(7)
            router(8)
            pe.wait_ge(sem["a_ok"], 1)
            b = claim(MD, md, "md_free")
            nc.tensor.matmul(b[:, 0:NE], tri[:, :], aa[:, 0, :], start=True, stop=True)
            nc.tensor.matmul(b[:, NE:NT * NE], tri[:, :], aa[:, 1:NT, :].rearrange("p i e -> p (i e)"), start=True, stop=False)
            nc.tensor.matmul(b[:, NE:NT * NE], ones[:, :], ac[:, 0:NT - 1, :].rearrange("p i e -> p (i e)"), start=False, stop=True)
            nc.tensor.matmul(b[:, NT * NE:NT * NE + NE], ones[:, :], ac[:, NT - 1, :], start=True, stop=True).then_inc(sem["md_full"], 1)
            pe.wait_ge(sem["r48_ok"], 1)
            b = claim(MD, md, "md_free")
            for i in range(NT):
                pe.wait_ge(sem["ro_ok"], i + 1)
                for c in range(2):
                    last = nc.tensor.matmul(b[:, 0:SLOTS], ro[i % 8][:, c, :], r48[:, i, c, :], start=i == 0 and c == 0, stop=i == NT - 1 and c == 1)
                last.then_inc(sem["md_full"], 1)

            def ew_gu(b):
                return ew[b][:, 0:4096].rearrange("p (k n) -> p k n", k=KD)

            def rows_t(b, ready, need, full, free):
                pe.wait_ge(sem[ready], need)
                for hf in range(2):
                    if free is not None:
                        pe.wait_ge(sem["t_free"], free + hf)
                    for k in range(4):
                        c = (hf * 4 + k) * P
                        last = nc.tensor.transpose(bank[hf][:, k * P:k * P + P], xg[b][:, c:c + P], ident[:, :])
                    last.then_inc(sem[full], 1)

            def gate_up(b, full):
                for k in range(KD):
                    last = nc.tensor.matmul(bank[2 + b % 2][:, :], xgt[b % 2][:, k, :], ew_gu(b)[:, k, :], start=k == 0, stop=k == KD - 1)
                last.then_inc(sem[full], 1)

            def prod_t(b, full):
                for k in range(2):
                    last = nc.tensor.transpose(bank[6 + b % 2][:, k * P:k * P + P], hpr[b % 2][:, k * P:k * P + P], ident[:, :])
                last.then_inc(sem[full], 1)

            def down(b, full):
                dn = ew[b][:, 4096:6144].rearrange("p (k n) -> p k n", k=2)
                for nh in range(2):
                    for k in range(2):
                        last = nc.tensor.matmul(bank[4 + nh][:, :], htr[b % 2][:, k, :], dn[:, k, nh * 512:nh * 512 + 512], start=k == 0, stop=k == 1)
                last.then_inc(sem[full], 1)

            def expert(e, b, r, ahead):
                if ahead > 1:
                    rows_t((b + 2) % 4, f"xg_in{(b + 2) % 4}", (r + ((b + 2) // 4 + 1)) * 16, "t_full", e * 2 + 3)
                pe.wait_ge(sem["prod_ok"], e + 1)
                prod_t(b, "ht_full")
                if ahead > 0:
                    n = (b + 1) % 4
                    pe.wait_ge(sem[f"ew_in{n}"], (r + (b + 1) // 4 + 1) * 48)
                    pe.wait_ge(sem["t_free"], e * 2 + 4)
                    gate_up(n, "gu_full")
                pe.wait_ge(sem["htm_ok"], e + 1)
                if not (isinstance(e, int) and e == 0):
                    pe.wait_ge(sem["ya_ok"], e)
                    pe.wait_ge(sem["yd_done"], e)
                down(b, "d_full")

            pe.wait_ge(sem["md_free"], 38)
            rows_t(0, "xg_in0", 16, "t_full", None)
            rows_t(1, "xg_in1", 16, "t_full", 1)
            pe.wait_ge(sem["ew_in0"], 48)
            pe.wait_ge(sem["t_free"], 2)
            gate_up(0, "gu_full")
            for b in range(4):
                expert(b, b, 0, 2)
            with pe.Fori(1, NE // 4 - 1) as r:
                for b in range(4):
                    expert(r * 4 + b, b, r, 2)
            for b in range(4):
                expert(NE - 4 + b, b, NE // 4 - 1, min(2, 3 - b))
            pe.wait_ge(sem["ctl_ok"], 1)
            with pe.If(pe.value_load(ctl[0:1, 16:17], min_val=0, max_val=16) > 0):
                with pe.Fori(0, 16) as i:
                    rows_t(0, "xg_in", (i + 1) * 16, "xt_full", None)
                    pe.wait_ge(sem["xw_in"], (i + 1) * 48)
                    pe.wait_ge(sem["xt_free"], i * 2 + 2)
                    gate_up(0, "xgu_full")
                    pe.wait_ge(sem["xprod_ok"], i + 1)
                    prod_t(0, "xht_full")
                    pe.wait_ge(sem["xhtm_ok"], i + 1)
                    down(0, "xd_full")

        @block.scalar
        def _(act):
            own = Count()
            ma, ta = Count(), Count()

            def link(ins):
                ins.then_inc(sem["act_own"], 1)
                act.wait_ge(sem["act_own"], own.next() + 1)

            act.wait_ge(sem["ident_ok"], 1)

            def square(n):
                r = P if n < MT else ROWS[n - MT]
                act.wait_ge(sem[f"x_in{n % 3}"], 16 * (n // 3 + 1))
                link(nc.scalar.activation(squares[0:r, :], xst[n % 3][0:r, :], ACT.Square, accum_out=ssq[0:r, n:n + 1]))
                nc.scalar.activation(rstd[0:r, n:n + 1], ssq[0:r, n:n + 1], ACT.Sqrt, scale=1.0 / D, bias=zero1[0:r, 1:2]).then_inc(sem["std_ok"], 1)

            def drain(ring, count, full, out, w, func, free, **kw):
                n = count.next()
                act.wait_ge(sem[full], n + 1)
                nc.scalar.activation(out, bank[ring[n % 2]][0:out.shape[0], 0:w] if isinstance(w, int) else w(bank[ring[n % 2]]), func, **kw).then_inc(sem[free], 1)

            for n in range(5):
                square(n)
            for hf in range(2):
                for m in range(MT):
                    drain(MA, ma, "ma_full", kst[:, m, hf * 512:hf * 512 + 512], 512, ACT.Copy, "ma_free")
            for n in range(5, 8):
                square(n)
            for hf in range(2):
                for m in range(MT):
                    drain(MA, ma, "ma_full", vv[:, m, hf * 512:hf * 512 + 512], 512, ACT.Copy, "ma_free")
            for n in range(8, NT + MT):
                square(n)
            act.wait_ge(sem["lam_in"], 48)
            nc.scalar.activation(ptmp[0:GP, 256:258], ptmp[0:GP, 256:258], ACT.Exp).then_inc(sem["dt_ok"], 1)
            act.wait_ge(sem["par_ok"], 2)
            nc.scalar.activation(spt[:, 4:8], spt[:, 0:4], ACT.Exp, scale=-1.0).then_inc(sem["spx_ok"], 1)
            act.wait_ge(sem["ang_ok"], 1)
            nc.scalar.activation(q16[0:GP, 6, :], q16[0:GP, 4, :], ACT.Exp).then_inc(sem["trig_ok"], 1)
            nc.scalar.activation(q16[0:GP, 9, :], q16[0:GP, 8, :], ACT.Sin).then_inc(sem["trig_ok"], 1)
            nc.scalar.activation(q16[0:GP, 10, :], q16[0:GP, 7, :], ACT.Sin).then_inc(sem["trig_ok"], 1)
            act.wait_ge(sem["ma_full"], 8)
            for c0, w in CHUNKS:
                for m in range(CT):
                    if c0 < SEQ:
                        drain(MA, ma, "ma_full", xl[:, m, 3 + c0:3 + c0 + w], w, ACT.Copy, "ma_free")
                    else:
                        drain(MA, ma, "ma_full", xl[:, m, 3 + SEQ:].rearrange("p (s t) -> p s t", s=NB)[:, :, 3:],
                              lambda bk: bk[:, 0:NB * DS].rearrange("p (s t) -> p s t", s=NB), ACT.Copy, "ma_free")
            for c0, w in CHUNKS:
                for m in range(CT):
                    drain(MA, ma, "ma_full", ut[:, m, :].rearrange("p (t k) -> p t k", t=L)[:, :, c0 // L:(c0 + w) // L],
                          lambda bk: bk[:, 0:w].rearrange("p (k t) -> p t k", t=L), ACT.Copy, "ma_free")
            act.wait_ge(sem["tp_full"], G_TP0 + 8)
            act.wait_ge(sem["h_ok"], 1)
            for q in range(4):
                for l in range(2):
                    n = ta.next()
                    act.wait_ge(sem["ta_full"], n + 1)
                    nc.scalar.activation(klag[0:GC, q * 4:q * 4 + 4, l, :], bank[TA[n % 2]][0:GC, :].rearrange("p (j n) -> p j n", j=4), ACT.Copy).then_inc(sem["ta_free"], 1)
                    act.wait_ge(sem["ta_free"], n + 1)
                    nc.scalar.nop().then_inc(sem["klag_ok"], 1)
            act.wait_ge(sem["klag_out"], 16)

            def glu_gate(chunks):
                for c0, w in chunks:
                    for m in range(CT):
                        drain(MA, ma, "ma_full", gl[:, m, c0:c0 + w], w, ACT.Gelu_apprx_tanh, "ma_free")

            glu_gate(CHUNKS[0:1])
            act.wait_ge(sem["small_ok"], 1)
            for gp in range(GP):
                drain(MA, ma, "ma_full", st[:, :, gp, :], lambda bk: bk[:, 0:2 * CS].rearrange("p (r k) -> p r k", r=2), ACT.Copy, "ma_free")
            glu_gate(CHUNKS[1:])

            def lru_gates(c):
                tr, ti, ts_ = lru_w[c % 2]
                if c == 1:
                    act.wait_ge(sem["end_ok"], 1)
                if c >= 2:
                    act.wait_ge(sem["ylru_ok"], c - 1)
                for a, dst in enumerate((tr, ti)):
                    for c0, w in CHUNKS:
                        bias = par[:, COL[("lru_b_a", "lru_b_x")[a]] + c:][:, 0:1]
                        drain(MA, ma, "ma_full", dst[:, c0:c0 + w], w, ACT.Sigmoid, "ma_free", bias=bias)
                act.wait_ge(sem["ma_free"], ma.n + 1)
                link(nc.scalar.activation(ts_[:, :], tr[:, :], ACT.Tanh, scale=m4sp[:, c:c + 1]))
                nc.scalar.activation(tr[:, :], tr[:, :], ACT.Exp, scale=m8sp[:, c:c + 1]).then_inc(sem["te_ok"], 1)

            def lru_root(c):
                ts_ = lru_w[c % 2][2]
                act.wait_ge(sem["sqrt_arg"], c + 1)
                nc.scalar.activation(ts_[:, :], ts_[:, :], ACT.Sqrt, scale=-1.0).then_inc(sem["sq_ok"], 1)

            def s5_out(g0, g1):
                for g in range(g0, g1):
                    n = ta.next()
                    act.wait_ge(sem["ta_full"], n + 1)
                    nc.scalar.activation(uch[:, g, :], bank[TA[n % 2]][:, 0:CS], ACT.Copy).then_inc(sem["ta_free"], 1)

            act.wait_ge(sem["spx_ok"], 2)
            lru_gates(0)
            s5_out(0, 4)
            lru_root(0)
            s5_out(4, GRP // 2)
            lru_gates(1)
            s5_out(GRP // 2, GRP // 2 + 4)
            lru_root(1)
            s5_out(GRP // 2 + 4, GRP // 2 + 8)
            lru_gates(2)
            s5_out(GRP // 2 + 8, GRP - 4)
            lru_root(2)
            s5_out(GRP - 4, GRP)
            lru_gates(3)
            lru_root(3)
            for c in range(CT):
                act.wait_ge(sem["ydc_ok"], c + 1)
                nc.scalar.activation(yd[:, c, :], yd[:, c, :], ACT.Gelu_apprx_tanh).then_inc(sem["yg_ok"], 1)
            for j, (t0, t1) in enumerate(TSPLIT):
                for m in range(CT):
                    i = j * CT + m
                    if i >= 2:
                        act.wait_ge(sem["ys5_ok"], i - 1)
                    drain(MA, ma, "ma_full", sig[i % 2][:, 0:(t1 - t0) * CS], (t1 - t0) * CS, ACT.Sigmoid, "ma_free",
                          bias=par[:, COL["s5_b_glu"] + m:COL["s5_b_glu"] + m + 1])

            def square2(i, done, squares_):
                r = ROWS[i]
                act.wait_ge(sem["md_free"], 2 * done + 2 * i + 2)
                link(nc.scalar.activation(squares_[0:r, :], xres[0:r, i, :], ACT.Square, accum_out=ssq[0:r, i:i + 1]))
                nc.scalar.activation(rstd[0:r, i:i + 1], ssq[0:r, i:i + 1], ACT.Sqrt, scale=1.0 / D, bias=zero1[0:r, 1:2]).then_inc(sem["sq2_ok"], 1)

            for i in range(NT):
                square2(i, 0, squares2)
            for c0, w in CHUNKS:
                for m in range(KD):
                    drain(MA, ma, "ma_full", qq[:, m, c0:c0 + w], w, ACT.Copy, "ma_free")

            def exps(s):
                for j in range(2):
                    act.wait_ge(sem["mx_ok"], 2 * s + j + 1)
                    if s >= 2 and j == 0:
                        act.wait_ge(sem["tp_full"], TP_P + 2 + (7 * (s - 2) - 1 if s > 2 else 0))
                    n = ta.next()
                    for t in range(2):
                        q_ = (2 * s + j) % 4 * 2 + t
                        ins = nc.scalar.activation(prob[s % 2][:, 2 * j + t, :], bank[TA[n % 2]][:, t * NM:t * NM + NM], ACT.Exp,
                                                   scale=XD ** -0.5, bias=smx[:, q_:q_ + 1], accum_out=srs[:, q_:q_ + 1])
                        if t == 0:
                            link(ins)
                    ins.then_inc(sem["ta_free"], 1)

            def sample_out(s):
                drain(MA, ma, "ma_full", h2[:, :, SEQ + DS * s:SEQ + DS * s + DS],
                      lambda bk: bk[:, 0:KD * DS].rearrange("p (k t) -> p k t", k=KD), ACT.Copy, "ma_free")

            exps(0)
            for s in range(8):
                if s + 1 < 8:
                    exps(s + 1)
                for d in range(2):
                    drain(MA, ma, "ma_full", h2[:, 2 * (s % XH) + d, 512 * (s // XH):512 * (s // XH) + 512], 512, ACT.Copy, "ma_free")
                if s >= 1:
                    sample_out(s - 1)
                act.wait_ge(sem["smx_ok"], s + 1)
                n = ta.next()
                nc.scalar.activation(probs[s % 2][:, :], bank[TA[n % 2]][:, 0:NM], ACT.Exp, scale=XD ** -0.5,
                                     bias=smx[:, 8 + s:9 + s], accum_out=srs[:, 8 + s:9 + s]).then_inc(sem["ta_free"], 1)
            sample_out(NB - 1)
            act.wait_ge(sem["consts_ok"], 1)
            for i in range(NT + 2):
                if i < NT:
                    square2(i, NT, squares3)
                if i >= 2:
                    drain(MA, ma, "ma_full", lg[0:ROWS[i - 2], i - 2, :], NG + NE, ACT.Copy, "ma_free")
            act.wait_ge(sem["lg_ok"], 1)
            nc.scalar.activation(g8[:, :, 4:8], g8[:, :, 0:4], ACT.Exp).then_inc(sem["gexp_ok"], 1)
            act.wait_ge(sem["edif_ok"], 1)
            nc.scalar.activation(cm(1)[:, 0:NT], cm(0)[:, 0:NT], ACT.Exp).then_inc(sem["eexp_ok"], 1)

            def silu(b, done):
                nc.scalar.activation(hsil[b % 2][:, :], bank[2 + b % 2][:, 0:FF], ACT.Silu).then_inc(sem[done], 1)

            def prod_copy(b, done):
                nc.scalar.activation(htr[b % 2][:, :, :].rearrange("p k t -> p (k t)"), bank[6 + b % 2][:, 0:FF], ACT.Copy).then_inc(sem[done], 1)

            def y_first(b, done):
                nc.scalar.activation(yst[b % 2][:, 0:512], bank[4][:, :], ACT.Copy).then_inc(sem[done], 1)

            def expert(e, b, r, more):
                first = isinstance(e, int)
                act.wait_ge(sem["ht_full"], e + 1)
                if not (first and e < 2):
                    act.wait_ge(sem["d_full"], e - 1)
                prod_copy(b, "htm_ok")
                if more:
                    act.wait_ge(sem["gu_full"], e + 2)
                    if not (first and e < 1):
                        act.wait_ge(sem["prod_ok"], e)
                    silu(b + 1, "silu_ok")
                act.wait_ge(sem["d_full"], e + 1)
                if not (first and e < 2):
                    act.wait_ge(sem[f"y_st{b % 2}"], (r * 2 + b // 2) * 16)
                y_first(b, "ya_ok")

            act.wait_ge(sem["gu_full"], 1)
            silu(0, "silu_ok")
            for b in range(4):
                expert(b, b, 0, True)
            with act.Fori(1, NE // 4 - 1) as r:
                for b in range(4):
                    expert(r * 4 + b, b, r, True)
            for b in range(4):
                expert(NE - 4 + b, b, NE // 4 - 1, b < 3)
            act.wait_ge(sem["ctl_ok"], 1)
            with act.If(act.value_load(ctl[0:1, 16:17], min_val=0, max_val=16) > 0):
                with act.Fori(0, 16) as i:
                    act.wait_ge(sem["xgu_full"], i + 1)
                    silu(0, "xsilu_ok")
                    act.wait_ge(sem["xht_full"], i + 1)
                    prod_copy(0, "xhtm_ok")
                    act.wait_ge(sem["xd_full"], i + 1)
                    y_first(0, "xya_ok")
            for i in range(NT):
                r = ROWS[i]
                act.wait_ge(sem["f_sum"], i + 1)
                link(nc.scalar.activation(squaresf[0:r, :], xres[0:r, i, :], ACT.Square, accum_out=ssq[0:r, i:i + 1]))
                nc.scalar.activation(rstd[0:r, i:i + 1], ssq[0:r, i:i + 1], ACT.Sqrt, scale=1.0 / D, bias=zero1[0:r, 1:2]).then_inc(sem["f_std"], 1)

        @block.vector
        def _(dve):
            own = Count()
            tp, md = Count(), Count()
            V = nc.vector

            def link(*ins):
                for i in ins:
                    i.then_inc(sem["dve_own"], 1)
                    own.next()
                dve.wait_ge(sem["dve_own"], own.n + 1)

            def cmul(o, a, b, t):
                link(V.tensor_tensor(o[0], a[0], b[0], MUL), V.tensor_tensor(t[0], a[1], b[1], MUL),
                     V.tensor_tensor(o[1], a[0], b[1], MUL), V.tensor_tensor(t[1], a[1], b[0], MUL))
                link(V.tensor_tensor(o[0], o[0], t[0], SUB), V.tensor_tensor(o[1], o[1], t[1], ADD))

            def full():
                n = tp.next()
                dve.wait_ge(sem["tp_full"], n + 1)
                return bank[TP[n % 2]]

            b = full()
            V.tensor_copy(par[:, 0:NVEC], b[:, 0:NVEC]).then_inc(sem["dve_own"], 1)
            own.next()
            V.tensor_copy(par[:, 136:232], b[:, 136:232]).then_inc(sem["tp_free"], 1)
            dve.wait_ge(sem["dve_own"], own.n + 1)
            dve.wait_ge(sem["tp_free"], 1)
            lam = par[:, COL["lru_lam"]:COL["lru_lam"] + 4]
            V.tensor_scalar(spt[:, 20:24], lam, -1.0, 0.0, MUL, ALU.max).then_inc(sem["par_ok"], 1)
            V.scalar_tensor_tensor(spt[:, 0:4], lam, -1.0, lam, MUL, ALU.max).then_inc(sem["par_ok"], 1)

            def xn(n):
                r = P if n < MT else ROWS[n - MT]
                dve.wait_ge(sem["std_ok"], n + 1)
                link(V.reciprocal(rstd[0:r, n:n + 1], rstd[0:r, n:n + 1]))
                V.tensor_scalar(xst[n % 3][0:r, :], xst[n % 3][0:r, :], rstd[0:r, n:n + 1], None, MUL).then_inc(sem["xn_ok"], 1)

            def gain(col, r, out_cols):
                for hf in range(2):
                    b = full()
                    V.tensor_tensor(out_cols(hf), b[:, :].rearrange("p (k t) -> p k t", k=4)[:, :, 0:r],
                                    par[:, col + 4 * hf:col + 4 * hf + 4].unsqueeze(2).to_broadcast([P, 4, r]), MUL).then_inc(sem["tp_free"], 1)

            def evac(n):
                if n < MT:
                    gain(COL["g_mem"], P, lambda hf: mt_[:, 4 * hf:4 * hf + 4, n * P:n * P + P])
                else:
                    i = n - MT
                    gain(COL["g_mix"], ROWS[i], lambda hf: ht[:, 4 * hf:4 * hf + 4, i * P:i * P + ROWS[i]])

            xn(0)
            for n in range(NT + MT):
                if n + 1 < NT + MT:
                    xn(n + 1)
                evac(n)
                if n == 4:
                    for m in range(MT):
                        for hf in range(2):
                            b = full()
                            V.tensor_copy(kt[:, 4 * hf:4 * hf + 4, m * P:m * P + P], b[:, :].rearrange("p (k t) -> p k t", k=4)).then_inc(sem["tp_free"], 1)

            dve.wait_ge(sem["spx_ok"], 1)
            z, s_, s2, acc = spt[:, 4:8], spt[:, 8:12], spt[:, 12:16], spt[:, 16:20]
            link(V.tensor_scalar(s_, z, 2.0, None, ADD))
            link(V.reciprocal(s_, s_))
            link(V.tensor_tensor(s_, s_, z, MUL))
            link(V.tensor_tensor(s2, s_, s_, MUL))
            link(V.tensor_scalar(acc, s2, 1.0 / 17, 1.0 / 15, MUL, ADD))
            for d in (13, 11, 9, 7, 5, 3, 1):
                link(V.tensor_tensor(acc, acc, s2, MUL))
                link(V.tensor_scalar(acc, acc, 1.0 / d, None, ADD))
            link(V.scalar_tensor_tensor(acc, acc, 2.0, s_, MUL, MUL))
            link(V.tensor_tensor(acc, acc, spt[:, 20:24], ADD))
            link(V.tensor_scalar(m4sp[:, :], acc, -4.0, None, MUL))
            V.tensor_scalar(m8sp[:, :], acc, -8.0, None, MUL).then_inc(sem["spx_ok"], 1)

            q = [q16[0:GP, j, :] for j in range(20)]
            q3 = [a.rearrange("p (l n) -> p l n", l=2) for a in q]
            dtb = ptmp[0:GP, 256:258].unsqueeze(2).to_broadcast([GP, 2, GN])
            dve.wait_ge(sem["dt_ok"], 1)
            dve.wait_ge(sem["lam_in"], 48)
            link(V.tensor_tensor(q3[4], q3[2], dtb, MUL), V.tensor_tensor(q3[5], q3[3], dtb, MUL))
            link(V.tensor_scalar(q[7], q[5], 1.0 / TWO_PI, ROUND, MUL, ADD))
            link(V.tensor_scalar(q[7], q[7], ROUND, None, SUB))
            link(V.scalar_tensor_tensor(q[8], q[7], -PI_HI, q[5], MUL, ADD))
            link(V.scalar_tensor_tensor(q[8], q[7], -PI_MID, q[8], MUL, ADD))
            link(V.scalar_tensor_tensor(q[8], q[7], -PI_LO, q[8], MUL, ADD))
            link(V.tensor_scalar(q[8], q[8], 3.1415925, -3.1415925, ALU.min, ALU.max))
            link(V.scalar_tensor_tensor(q[7], q[8], -1.0, q[8], MUL, ALU.min))
            V.tensor_scalar(q[7], q[7], math.pi / 2, None, ADD).then_inc(sem["ang_ok"], 1)
            dve.wait_ge(sem["trig_ok"], 3)
            link(V.tensor_tensor(q[11], q[6], q[10], MUL), V.tensor_tensor(q[12], q[6], q[9], MUL),
                 V.tensor_tensor(q[18], q[2], q[2], MUL), V.tensor_tensor(q[19], q[3], q[3], MUL))
            link(V.tensor_tensor(q[18], q[18], q[19], ADD))
            link(V.reciprocal(q[18], q[18]))
            link(V.scalar_tensor_tensor(q[13], q[11], -1.0, q[2], ADD, MUL), V.tensor_tensor(q[19], q[12], q[3], MUL))
            link(V.tensor_tensor(q[13], q[13], q[19], ADD))
            link(V.tensor_tensor(q[13], q[13], q[18], MUL))
            link(V.tensor_tensor(q[14], q[12], q[2], MUL), V.scalar_tensor_tensor(q[19], q[11], -1.0, q[3], ADD, MUL))
            link(V.tensor_tensor(q[14], q[14], q[19], SUB))
            link(V.tensor_tensor(q[14], q[14], q[18], MUL))
            link(V.tensor_copy(q[15], q[10]), V.tensor_copy(q[16], q[9]), V.tensor_copy(q[17], q[6]))
            for _ in range(int(math.log2(L))):
                link(V.tensor_tensor(q[18], q[15], q[15], MUL), V.tensor_tensor(q[19], q[16], q[16], MUL), V.tensor_tensor(q[17], q[17], q[17], MUL))
                link(V.scalar_tensor_tensor(q[16], q[15], 2.0, q[16], MUL, MUL))
                link(V.tensor_tensor(q[15], q[18], q[19], SUB))
            link(V.tensor_tensor(q[18], q[15], q[15], MUL), V.tensor_tensor(q[19], q[16], q[16], MUL))
            link(V.tensor_tensor(q[18], q[18], q[19], ADD))
            link(V.tensor_scalar(q[18], q[18], -0.5, 1.5, MUL, ADD))
            link(V.tensor_tensor(q[15], q[15], q[18], MUL))
            V.tensor_tensor(q[16], q[16], q[18], MUL).then_inc(sem["scal_ok"], 1)

            b = full()
            V.tensor_copy(sp7[:, :, :], b[:, 0:7 * GP].rearrange("p (j g) -> p j g", j=7)).then_inc(sem["tp_free"], 1)
            dve.wait_ge(sem["tp_free"], tp.n + 1)
            dve.wait_ge(sem["ma_full"], 8)
            for ri in range(2):
                b = full()
                bv = b[:, :].rearrange("p (g l c) -> p g l c", l=2, c=GC)
                link(V.tensor_copy(cnat[0:64, ri, :, :], bv[0:64, :, 0, :]))
                V.tensor_copy(cnat[64:128, ri, :, :], bv[64:128, :, 1, :]).then_inc(sem["tp_free"], 1)
            b = full()
            V.tensor_copy(h0t[:, :, :, :], b[:, 0:256].rearrange("p (r s g) -> p r s g", r=2, s=NB)).then_inc(sem["tp_free"], 1)
            dve.wait_ge(sem["tp_free"], tp.n + 1)
            link(V.memset(pw[:, 0, 0, :], 1.0), V.memset(pw[:, 1, 0, :], 0.0), V.tensor_copy(pw[:, :, 1, :], sp7[:, 0:2, :]))
            for m in (1, 2, 4):
                cmul([pw[:, r, m + 1:2 * m + 1, :] for r in range(2)], [pw[:, r, 1:m + 1, :] for r in range(2)],
                     [pw[:, r, m:m + 1, :].to_broadcast([P, m, GP]) for r in range(2)],
                     [ptmp[:, 64 * r:64 * r + 16 * m].rearrange("p (m g) -> p m g", m=m) for r in range(2)])
            dve.wait_ge(sem["bnat_in"], 16 * 18)
            cmul([bbar[:, r, :, :] for r in range(2)], [bnat[:, r, :, :] for r in range(2)],
                 [sp7[:, 2 + r, :].unsqueeze(2).to_broadcast([P, GP, GC]) for r in range(2)],
                 [hmat[:, r, :, 0, :] for r in range(2)])
            dve.wait_ge(sem["kv_out"], 48)
            for h in range(GP // GH):
                gs = slice(h * GH, h * GH + GH)
                sh = [P, GH, L + 1, GC]
                cv = [cnat[:, r, gs, :].unsqueeze(2).to_broadcast(sh) for r in range(2)]
                pv = [pw[:, r, :, gs].rearrange("p t g -> p g t").unsqueeze(3).to_broadcast(sh) for r in range(2)]
                hr, hi = hmat[:, 0, gs, :, :], hmat[:, 1, gs, :, :]
                link(V.tensor_tensor(hr, cv[0], pv[0], MUL), V.tensor_tensor(htmp[:, :, :, :], cv[1], pv[1], MUL))
                link(V.tensor_tensor(hr, hr, htmp[:, :, :, :], SUB))
                link(V.tensor_tensor(hi, cv[0], pv[1], MUL), V.tensor_tensor(htmp[:, :, :, :], cv[1], pv[0], MUL))
                link(V.scalar_tensor_tensor(hi.rearrange("p g t c -> p (g t c)"), hi.rearrange("p g t c -> p (g t c)"), -1.0,
                                            htmp[:, :, :, :].rearrange("p g t c -> p (g t c)"), MUL, SUB))
            V.tensor_copy(spt[:, 0:1], spt[:, 0:1]).then_inc(sem["h_ok"], 1)
            def conv_and_phases():
                dve.wait_ge(sem["ma_free"], 20)
                xs = [xl[:, c, 3 + SEQ:].rearrange("p (s t) -> p s t", s=NB) for c in range(CT)]
                for c in range(CT):
                    link(V.memset(xl[:, c, 0:3], 0.0), V.tensor_copy(xs[c][:, :, 0:3], convst[:, :, :, c]))
                    link(V.tensor_copy(lc[:, 0, :, c], xl[:, c, SEQ:SEQ + 3]), V.tensor_copy(lc[:, 1:, :, c], xs[c][:, :, DS:DS + 3]))
                    xcs = xc[:, c, SEQ:].rearrange("p (s t) -> p s t", s=NB)
                    cw = [par[:, COL["lru_conv_w"] + 4 * k + c:COL["lru_conv_w"] + 4 * k + c + 1] for k in range(4)]
                    cb = par[:, COL["lru_conv_b"] + c:COL["lru_conv_b"] + c + 1]
                    link(V.tensor_scalar(xc[:, c, 0:SEQ], xl[:, c, 0:SEQ], cw[0], cb, MUL, ADD),
                         V.tensor_scalar(xcs, xs[c][:, :, 0:DS], cw[0], cb, MUL, ADD))
                    for k in range(1, 4):
                        a_ = V.scalar_tensor_tensor(xc[:, c, 0:SEQ], xl[:, c, k:k + SEQ], cw[k], xc[:, c, 0:SEQ], MUL, ADD)
                        b_ = V.scalar_tensor_tensor(xcs, xs[c][:, :, k:k + DS], cw[k], xcs, MUL, ADD)
                        link(a_, b_)
                    V.tensor_copy(spt[:, 0:1], spt[:, 0:1]).then_inc(sem["xc_ok"], 1)
                    dve.wait_ge(sem["xc_ok"], c + 1)

                dve.wait_ge(sem["kv_out"], 48)
                tab = [cost, sint]
                ph = [ptmp2[:, 16 * r:16 * r + 16] for r in range(2)]
                pt = [ptmp2[:, 32 + 16 * r:48 + 16 * r] for r in range(2)]
                p2 = [ptmp2[:, 64 + 16 * r:80 + 16 * r] for r in range(2)]
                link(V.memset(cost[:, :, 0:1], 1.0), V.memset(sint[:, :, 0:1], 0.0), V.tensor_copy(ph[0], sp7[:, 4, :]), V.tensor_copy(ph[1], sp7[:, 5, :]))
                k = 1
                while k < CK:
                    w = [st_flat[:, r * 1024:r * 1024 + GP * k].rearrange("p (g k) -> p g k", g=GP) for r in range(2)]
                    cmul([t[:, :, k:2 * k] for t in tab], [t[:, :, 0:k] for t in tab], [a.unsqueeze(2).to_broadcast([P, GP, k]) for a in ph], w)
                    cmul(p2, ph, ph, pt)
                    link(V.tensor_copy(ph[0], p2[0]), V.tensor_copy(ph[1], p2[1]))
                    k *= 2
                V.tensor_copy(spt[:, 0:1], spt[:, 0:1]).then_inc(sem["small_ok"], 1)

            for h in range(GP // GH):
                gs = slice(h * GH, h * GH + GH)
                sh = [P, GH, L, GC]
                bv = [bbar[:, r, gs, :].unsqueeze(2).to_broadcast(sh) for r in range(2)]
                pv = [pw[:, r, 0:L, gs].rearrange("p t g -> p g t").unsqueeze(3).to_broadcast(sh) for r in range(2)]
                if h == 1:
                    dve.wait_ge(sem["tp_full"], G_TP0 + 4)
                gr, gi = gnat[:, 0, :, :, :], gnat[:, 1, :, :, :]
                link(V.tensor_tensor(gr, bv[0], pv[0], MUL), V.tensor_tensor(gtmp[:, :, :, :], bv[1], pv[1], MUL))
                link(V.tensor_tensor(gr, gr, gtmp[:, :, :, :], SUB))
                link(V.tensor_tensor(gi, bv[0], pv[1], MUL), V.tensor_tensor(gtmp[:, :, :, :], bv[1], pv[0], MUL))
                V.tensor_tensor(gi, gi, gtmp[:, :, :, :], ADD).then_inc(sem["gnat_ok"], 1)
                dve.wait_ge(sem["gnat_ok"], h + 1)
                if h == 0:
                    conv_and_phases()
                for f in range(4):
                    b = full()
                    gp = h * GH + 2 * f
                    V.tensor_copy(gmat[:, gp:gp + 2, :, :].rearrange("p g r n -> p (g r n)"), b[:, :]).then_inc(sem["tp_free"], 1)

            dve.wait_ge(sem["u_out"], 16)
            dve.wait_ge(sem["ma_free"], 52)
            a8 = [pw[:, r, L, :].unsqueeze(1).to_broadcast([P, NB, GP]) for r in range(2)]
            sv = [st[:, r, :, CK:].rearrange("p g s -> p s g") for r in range(2)]
            w8 = [rot[r][:, 0, :].rearrange("p (s g) -> p s g", s=NB) for r in range(2)]
            cmul([fin[:, r, :, :] for r in range(2)], [h0t[:, r, :, :] for r in range(2)], a8, w8)
            link(V.tensor_tensor(fin[:, 0, :, :], fin[:, 0, :, :], sv[0], ADD), V.tensor_tensor(fin[:, 1, :, :], fin[:, 1, :, :], sv[1], ADD))
            for h in range(GP // GH):
                gs = slice(h * GH, h * GH + GH)
                s0, s1 = st[:, 0, gs, 0:CK], st[:, 1, gs, 0:CK]
                co, si = cost[:, gs, :], sint[:, gs, :]
                for sgn in (0, 1):
                    link(V.tensor_tensor(rot[0][:, :, :], s0, si, MUL), V.tensor_tensor(rot[1][:, :, :], s1, si, MUL))
                    link(V.tensor_tensor(s0, s0, co, MUL), V.tensor_tensor(s1, s1, co, MUL))
                    link(V.tensor_tensor(s0, s0, rot[1][:, :, :], (ADD, SUB)[sgn]), V.tensor_tensor(s1, s1, rot[0][:, :, :], (SUB, ADD)[sgn]))
                    if sgn == 0:
                        link(*[V.tensor_tensor_scan(st[:, r, g, 0:CK], sp7[:, 6, g:g + 1].to_broadcast([P, CK]), st[:, r, g, 0:CK], 0.0, MUL, ADD)
                               for g in range(h * GH, h * GH + GH) for r in range(2)])
            V.tensor_copy(finp[:, :, :], st[:, :, :, CK - 1]).then_inc(sem["end_ok"], 1)
            dve.wait_ge(sem["end_ok"], 1)
            link(V.tensor_copy(st[:, 0, :, CK - 1:CS - 1], h0t[:, 0, :, :].rearrange("p s g -> p g s")),
                 V.tensor_copy(st[:, 1, :, CK - 1:CS - 1], h0t[:, 1, :, :].rearrange("p s g -> p g s")))
            V.tensor_copy(spt[:, 0:1], spt[:, 0:1]).then_inc(sem["hs_ok"], 1)
            for c in range(CT):
                xcc = xc[:, c, :]
                tr, ti, ts_ = lru_w[c % 2]
                dve.wait_ge(sem["te_ok"], c + 1)
                link(V.tensor_tensor(xcc, xcc, ti[:, :], MUL), V.tensor_scalar(tr[:, :], tr[:, :], 0.5, 0.5, MUL, ADD))
                link(V.scalar_tensor_tensor(ti[:, :], ts_[:, :], -1.0, tr[:, :], ADD, MUL))
                link(V.scalar_tensor_tensor(tr[:, :], ti[:, :], 2.0, tr[:, :], ADD, MUL))
                V.scalar_tensor_tensor(ti[:, :], ts_[:, :], 1.0, tr[:, :], ADD, MUL).then_inc(sem["sqrt_arg"], 1)
                dve.wait_ge(sem["sq_ok"], c + 1)
                link(V.scalar_tensor_tensor(ts_[:, :], ts_[:, :], 2.0, tr[:, :], MUL, MUL))
                link(V.tensor_tensor(ts_[:, :], ts_[:, :], xcc, MUL))
                a0 = ti[:, SEQ:].rearrange("p (s t) -> p s t", s=NB)[:, :, 0]
                b0 = ts_[:, SEQ:].rearrange("p (s t) -> p s t", s=NB)[:, :, 0]
                hl = par[:, COL["state_lru_h"]:COL["state_lru_h"] + NB * CT].rearrange("p (s c) -> p s c", s=NB)[:, :, c]
                link(V.tensor_tensor(spt[:, 8:16], a0, hl, MUL))
                link(V.tensor_tensor(b0, b0, spt[:, 8:16], ADD), V.memset(a0, 0.0))
                link(V.tensor_tensor_scan(xcc, ti[:, :], ts_[:, :], 0.0, MUL, ADD))
                link(V.tensor_copy(lh[:, 0:1, c], xcc[:, SEQ - 1:SEQ]), V.tensor_copy(lh[:, 1:, c], xcc[:, SEQ:].rearrange("p (s t) -> p s t", s=NB)[:, :, DS - 1]))
                if c == 0:
                    dve.wait_ge(sem["ma_free"], 60)
                V.tensor_tensor(gl[:, c, :], gl[:, c, :], xcc, MUL).then_inc(sem["ylru_ok"], 1)
            V.tensor_copy(spt[:, 0:1], spt[:, 0:1]).then_inc(sem["lru_ends"], 1)

            b = full()
            link(V.tensor_copy(xl_t[0:36, 0:P], b[0:36, 0:P]))
            V.tensor_copy(xl_t[0:108, P:2 * P], b[0:108, P:2 * P]).then_inc(sem["tp_free"], 1)
            dve.wait_ge(sem["tp_free"], tp.n + 1)
            V.tensor_copy(spt[:, 0:1], spt[:, 0:1]).then_inc(sem["small_ok"], 1)
            b = full()
            link(V.tensor_copy(s5_t[:, 0:2, :], b[:, 0:2 * P].rearrange("p (j n) -> p j n", j=2)))
            V.tensor_copy(s5_t[0:GP, 2:4, :], b[0:GP, 2 * P:].rearrange("p (j n) -> p j n", j=2)).then_inc(sem["tp_free"], 1)
            dve.wait_ge(sem["tp_free"], tp.n + 1)
            V.tensor_copy(spt[:, 0:1], spt[:, 0:1]).then_inc(sem["small_ok"], 1)

            dve.wait_ge(sem["y_in"], 16)
            dve.wait_ge(sem["ut_in"], 16)
            for c in range(CT):
                V.scalar_tensor_tensor(yd[:, c, :], ut[:, c, :], par[:, COL["s5_d"] + c:COL["s5_d"] + c + 1], yd[:, c, :], MUL, ADD).then_inc(sem["ydc_ok"], 1)
            dve.wait_ge(sem["yg_ok"], CT)
            for j, (t0, t1) in enumerate(TSPLIT):
                for m in range(CT):
                    i = j * CT + m
                    dve.wait_ge(sem["ma_free"], 84 + i + 1)
                    w = (t1 - t0) * CS
                    V.tensor_tensor(ut[:, m, :].rearrange("p (k t) -> p t k", t=L)[:, t0:t1, :],
                                    yd[:, m, t0 * CS:t1 * CS].rearrange("p (t k) -> p t k", k=CS),
                                    sig[i % 2][:, 0:w].rearrange("p (t k) -> p t k", k=CS), MUL).then_inc(sem["ys5_ok"], 1)

            def resid(i, done):
                r = ROWS[i]
                if done == 0:
                    dve.wait_ge(sem[f"x_res{i // 4}"], 16)
                for nh in range(2):
                    n = md.next()
                    dve.wait_ge(sem["md_full"], n + 1)
                    xs_ = xres[0:r, i, nh * 512:nh * 512 + 512]
                    V.tensor_tensor(xs_, xs_, bank[MD[n % 2]][0:r, :], ADD).then_inc(sem["md_free"], 1)
                dve.wait_ge(sem["sq2_ok"], done + i + 1)
                link(V.reciprocal(rstd[0:r, i:i + 1], rstd[0:r, i:i + 1]))
                if i >= 2:
                    dve.wait_ge(sem["tp_full"], (TP_M if done else TP_XA) + 2 * (i - 1))
                    if done:
                        dve.wait_ge(sem[f"xn2_st{i % 2}"], 16 * (i // 2))
                V.tensor_scalar(xns[i % 2][0:r, :], xres[0:r, i, :], rstd[0:r, i:i + 1], None, MUL).then_inc(sem["xn2_ok"], 1)

            def gain2(i, col):
                gain(COL[col], ROWS[i], lambda hf: h2[:, 4 * hf:4 * hf + 4, i * P:i * P + ROWS[i]])

            for i in range(NT):
                resid(i, 0)
                if i >= 1:
                    gain2(i - 1, "g_xa")
            gain2(NT - 1, "g_xa")

            taf = Count()
            taf.n = Y_TA0 + GRP - 1

            def maxima(s):
                fills = []
                for j in range(2):
                    n = taf.next()
                    fills.append(n + 1)
                    dve.wait_ge(sem["ta_full"], n + 1)
                    q_ = (2 * s + j) % 4 * 2
                    link(V.tensor_reduce(smx[:, q_:q_ + 2], bank[TA[n % 2]][:, :].rearrange("p (t m) -> p t m", t=2), AX.X, ALU.max))
                    V.tensor_scalar(smx[:, q_:q_ + 2], smx[:, q_:q_ + 2], -(XD ** -0.5), None, MUL).then_inc(sem["mx_ok"], 1)
                return fills

            def shares(s, fills):
                for j in range(2):
                    q_ = (2 * s + j) % 4 * 2
                    dve.wait_ge(sem["ta_free"], fills[j])
                    link(V.reciprocal(srs[:, q_:q_ + 2], srs[:, q_:q_ + 2]))
                    pj = prob[s % 2][:, 2 * j:2 * j + 2, :]
                    V.tensor_tensor(pj, pj, srs[:, q_:q_ + 2].unsqueeze(2).to_broadcast([P, 2, NM]), MUL).then_inc(sem["pn_ok"], 1)

            def cache_k():
                for m in range(MT):
                    for hf in range(2):
                        b = full()
                        V.tensor_copy(ktb[:, 4 * hf:4 * hf + 4, m * P:m * P + P], b[:, :].rearrange("p (k t) -> p k t", k=4)).then_inc(sem["tp_free"], 1)

            def sample_pts():
                b = full()
                V.tensor_copy(pts[:, :, :], b[:, 0:2 * P].rearrange("p (m c) -> p m c", m=2)).then_inc(sem["tp_free"], 1)

            shares(0, maxima(0))
            for s in range(8):
                for j in range(2):
                    b = full()
                    V.tensor_copy(ptr[:, :, j * 256:j * 256 + 256].rearrange("p m (t c) -> p t m c", t=2),
                                  b[:, :].rearrange("p (t m c) -> p t m c", t=2, m=2)).then_inc(sem["tp_free"], 1)
                cache_k()
                if s >= 1:
                    sample_pts()
                if s + 1 < 8:
                    shares(s + 1, maxima(s + 1))
                mx_, rs_ = smx[:, 8 + s:9 + s], srs[:, 8 + s:9 + s]
                n = taf.next()
                dve.wait_ge(sem["ta_full"], n + 1)
                link(V.tensor_reduce(mx_, bank[TA[n % 2]][:, 0:NM], AX.X, ALU.max))
                V.tensor_scalar(mx_, mx_, -(XD ** -0.5), None, MUL).then_inc(sem["smx_ok"], 1)
                dve.wait_ge(sem["ta_free"], n + 1)
                link(V.reciprocal(rs_, rs_))
                V.tensor_scalar(probs[s % 2][:, :], probs[s % 2][:, :], rs_, None, MUL).then_inc(sem["spn_ok"], 1)
            sample_pts()

            for i in range(NT):
                resid(i, NT)
                if i >= 1:
                    gain2(i - 1, "g_moe")
            gain2(NT - 1, "g_moe")

            dve.wait_ge(sem["ma_free"], MA_R)
            dve.wait_ge(sem["ma_full"], MA_R)
            NEG = -3.0e38
            link(V.memset(g8[:, :, :], NEG))
            link(V.tensor_copy(g8[:, :, 0:4], lg[:, :, 0:NG]))
            link(*[V.max(m8[:, i, :], g8[:, i, :]) for i in range(NT)])
            link(*[V.max_index(i8[:, i, :], m8[:, i, :], g8[:, i, :]) for i in range(NT)])
            gs_, pgs = cm(2)[:, 0:NT], cm(3)[:, 0:NT]
            link(V.tensor_copy(gs_, i8[:, :, 0]))
            V.tensor_tensor(g8[:, :, 0:4], g8[:, :, 0:4], m8[:, :, 0:1].to_broadcast([P, NT, 4]), SUB).then_inc(sem["lg_ok"], 1)
            pen = otmp[:, :, 0, 0:4]
            link(V.tensor_tensor(pen, iota[:, 0:4].unsqueeze(1).to_broadcast([P, NT, 4]), gs_.unsqueeze(2).to_broadcast([P, NT, 4]), ALU.is_equal))
            link(V.tensor_scalar(pen, pen, 1.0, -NEG, SUB, MUL))
            link(V.tensor_tensor(le[:, :, :].rearrange("p i (g e) -> p i g e", g=NG), lg[:, :, NG:].rearrange("p i (g e) -> p i g e", g=NG),
                                 pen.unsqueeze(3).to_broadcast([P, NT, NG, NE // NG]), ADD))
            link(*[V.max(m8[:, i, :], le[:, i, :]) for i in range(NT)])
            V.tensor_tensor(cm(0)[:, 0:NT], m8[:, :, 1], m8[:, :, 0], SUB).then_inc(sem["edif_ok"], 1)
            dve.wait_ge(sem["lg_ok"], 1)
            link(*[V.max_index(i8[:, i, :], m8[:, i, :], le[:, i, :]) for i in range(NT)])
            eid = cm(4).rearrange("p (i c) -> p i c", c=2)
            link(V.tensor_copy(eid, i8[:, :, 0:2]))
            flat = lambda a: a.rearrange("p i c e -> p (i c) e")
            link(V.tensor_tensor(flat(oh[:, :, :, :]), iota[:, 0:NE].unsqueeze(1).to_broadcast([P, 2 * NT, NE]),
                                 cm(4).unsqueeze(2).to_broadcast([P, 2 * NT, NE]), ALU.is_equal))
            link(V.memset(oh[ROWS[8]:P, NT - 1, :, :], 0.0))
            link(V.tensor_tensor(aa[:, :, :], oh[:, :, 0, :], oh[:, :, 1, :], ADD))
            link(V.tensor_copy(ac[:, 0, :], aa[:, 0, :]))
            for i in range(1, NT - 1):
                link(V.tensor_tensor(ac[:, i, :], ac[:, i - 1, :], aa[:, i, :], ADD))
            V.tensor_tensor(ac[:, NT - 1, :], ac[:, NT - 2, :], aa[:, NT - 1, :], ADD).then_inc(sem["a_ok"], 1)
            dve.wait_ge(sem["gexp_ok"], 1)
            link(V.tensor_reduce(pgs, g8[:, :, 4:8], AX.X, ADD))
            dve.wait_ge(sem["eexp_ok"], 1)
            link(V.tensor_scalar(cm(6)[:, 0:NT], cm(1)[:, 0:NT], 1.0, None, ADD))
            link(V.tensor_tensor(pgs, pgs, cm(6)[:, 0:NT], MUL))
            link(V.reciprocal(wcomb[:, :, 0], pgs))
            link(V.tensor_tensor(wcomb[:, :, 1], wcomb[:, :, 0], cm(1)[:, 0:NT], MUL))
            n = md.next()
            dve.wait_ge(sem["md_full"], n + 1)
            b = bank[MD[n % 2]]
            link(V.tensor_tensor(otmp[:, :, :, :], oh[:, :, :, :], b[:, 0:NT * NE].rearrange("p (i e) -> p i e", e=NE).unsqueeze(2).to_broadcast([P, NT, 2, NE]), MUL))
            rk, ex, qn, tile = cm(6), cm(7), cm(8), cm(9)
            V.tensor_copy(cnt[:, 0, :], b[:, NT * NE:NT * NE + NE]).then_inc(sem["md_free"], 1)
            dve.wait_ge(sem["md_free"], n + 1)
            link(V.tensor_reduce(rk, flat(otmp[:, :, :, :]), AX.X, ADD), V.memset(cnt[:, 1, :], 0.0), V.memset(cnt[:, 3, :], 0.0), V.memset(qn, 0.0))
            for m in range(1, 9):
                link(V.scalar_tensor_tensor(cnt[:, 1, :], cnt[:, 0, :], float(P * m), cnt[:, 1, :], ALU.is_gt, ADD),
                     V.scalar_tensor_tensor(qn, rk, float(P * m), qn, ALU.is_ge, ADD))
            link(V.tensor_tensor_scan(cnt[:, 2, :], cnt[:, 1, :], cnt[:, 3, :], 0.0, ADD, ADD))
            link(V.tensor_tensor(cnt[:, 3, :], cnt[:, 2, :], cnt[:, 1, :], SUB))
            link(V.tensor_tensor(flat(otmp[:, :, :, :]), flat(oh[:, :, :, :]), cnt[:, 3, :].unsqueeze(1).to_broadcast([P, 2 * NT, NE]), MUL))
            link(V.tensor_reduce(ex, flat(otmp[:, :, :, :]), AX.X, ADD), V.scalar_tensor_tensor(rk, qn, float(-P), rk, MUL, ADD))
            link(V.scalar_tensor_tensor(ex, ex, float(NE - 1), qn, ADD, ADD))
            link(V.tensor_tensor(tile, cm(4), ex, SUB), V.tensor_scalar(qn, qn, 0.0, None, ALU.is_equal))
            link(V.tensor_tensor(tile, tile, qn, MUL))
            link(V.tensor_tensor(tile, tile, ex, ADD))
            r48f = r48[:, :, :, :].rearrange("p i c n -> p (i c) n")
            link(V.tensor_tensor(r48f, iota[:, 0:SLOTS].unsqueeze(1).to_broadcast([P, 2 * NT, SLOTS]), tile.unsqueeze(2).to_broadcast([P, 2 * NT, SLOTS]), ALU.is_equal))
            V.tensor_tensor(r48f, r48f, val[:, :, :].rearrange("p i c -> p (i c)").unsqueeze(2).to_broadcast([P, 2 * NT, SLOTS]), MUL).then_inc(sem["r48_ok"], 1)
            dve.wait_ge(sem["xn2_st0"], 80)
            dve.wait_ge(sem["xn2_st1"], 64)
            for i in range(NT):
                if i == 8:
                    dve.wait_ge(sem["md_full"], 38)
                V.tensor_tensor(ro[i % 8][:, :, :], iota[:, :].unsqueeze(1).to_broadcast([P, 2, P]),
                                rk.rearrange("p (i c) -> p i c", c=2)[:, i, :].unsqueeze(2).to_broadcast([P, 2, P]), ALU.is_equal).then_inc(sem["ro_ok"], 1)
            n = md.next()
            dve.wait_ge(sem["md_full"], 37 + NT)
            b = bank[MD[n % 2]]
            v_, w_ = otmp[:, 0:3, :, :].rearrange("p i c e -> p (i c e)")[:, 0:SLOTS], otmp[:, 3:6, :, :].rearrange("p i c e -> p (i c e)")[:, 0:SLOTS]
            V.tensor_scalar(v_, b[:, 0:SLOTS], 1.0, None, SUB).then_inc(sem["md_free"], 1)
            dve.wait_ge(sem["md_free"], 38)
            link(V.tensor_scalar(w_, v_, 0.0, 1.0e6, ALU.is_lt, MUL))
            link(V.tensor_tensor(v_, v_, w_, ADD))
            link(V.tensor_scalar(w_, v_, float(TOK), float(-TOK), ALU.is_ge, MUL))
            link(V.tensor_tensor(w_, v_, w_, ADD))
            link(V.tensor_copy(idxs[:, :], v_))
            V.tensor_copy(idxg[:, :], w_).then_inc(sem["idx_ok"], 1)
            dve.wait_ge(sem["ro_ok"], NT)
            dve.wait_ge(sem["md_full"], 37 + NT)
            link(V.tensor_tensor(ovt[0:1, :, :], cnt[0:1, 2, :].unsqueeze(1).to_broadcast([1, 16, NE]), iota[0:1, 0:16].unsqueeze(2).to_broadcast([1, 16, NE]), ALU.is_le))
            link(V.tensor_reduce(ovf[0:1, 0:16], ovt[0:1, :, :], AX.X, ADD), V.tensor_copy(ovf[0:1, 16:17], cnt[0:1, 2, NE - 1:NE]))
            link(V.tensor_scalar(ovf[0:1, 0:16], ovf[0:1, 0:16], float(NE - 1), None, ALU.min))
            V.tensor_copy(ctl[0:1, 0:17], ovf[0:1, 0:17]).then_inc(sem["ctl_ok"], 1)

            def rows(b, done):
                for hf in range(2):
                    dve.wait_ge(*done(hf))
                    V.tensor_tensor(xgt[b % 2][:, 4 * hf:4 * hf + 4, :], bank[hf][:, :].rearrange("p (k t) -> p k t", k=4),
                                    par[:, COL["g_moe"] + 4 * hf:COL["g_moe"] + 4 * hf + 4].unsqueeze(2).to_broadcast([P, 4, P]), MUL).then_inc(*done(2 + hf))

            def product(b, done):
                V.tensor_tensor(hpr[b % 2][:, :], hsil[b % 2][:, :], bank[2 + b % 2][:, FF:2 * FF], MUL).then_inc(sem[done], 1)

            def y_second(b, done):
                V.tensor_copy(yst[b % 2][:, 512:1024], bank[5][:, :]).then_inc(sem[done], 1)

            def main_rows(e, b):
                rows(b, lambda j: (sem["t_full"], e * 2 + (j + 1)) if j < 2 else (sem["t_free"], 1))

            def expert(e, b, r, ahead):
                first = isinstance(e, int)
                if ahead > 1:
                    dve.wait_ge(sem["gu_full"], e + 1)
                    main_rows(e + 2, b)
                if ahead > 0:
                    dve.wait_ge(sem["silu_ok"], e + 2)
                    if not (first and e < 1):
                        dve.wait_ge(sem["ht_full"], e)
                    product(b + 1, "prod_ok")
                dve.wait_ge(sem["d_full"], e + 1)
                if not (first and e < 2):
                    dve.wait_ge(sem[f"y_st{b % 2}"], (r * 2 + b // 2) * 16)
                y_second(b, "yd_done")

            main_rows(0, 0)
            main_rows(1, 1)
            dve.wait_ge(sem["silu_ok"], 1)
            product(0, "prod_ok")
            for b in range(4):
                expert(b, b, 0, 2)
            with dve.Fori(1, NE // 4 - 1) as r:
                for b in range(4):
                    expert(r * 4 + b, b, r, 2)
            for b in range(4):
                expert(NE - 4 + b, b, NE // 4 - 1, min(2, 3 - b))
            with dve.If(dve.value_load(ctl[0:1, 16:17], min_val=0, max_val=16) > 0):
                with dve.Fori(0, 16) as i:
                    rows(0, lambda j: (sem["xt_full"], i * 2 + (j + 1)) if j < 2 else (sem["xt_free"], 1))
                    dve.wait_ge(sem["xsilu_ok"], i + 1)
                    product(0, "xprod_ok")
                    dve.wait_ge(sem["xd_full"], i + 1)
                    y_second(0, "xyd_ok")

            def fsum(i):
                r = ROWS[i]
                dve.wait_ge(sem[f"f_in{i % 3}"], 32 * (i // 3 + 1))
                link(V.scalar_tensor_tensor(xres[0:r, i, :], fy[i % 3][0:r, 0, :], wcomb[0:r, i, 0:1], xres[0:r, i, :], MUL, ADD))
                V.scalar_tensor_tensor(xres[0:r, i, :], fy[i % 3][0:r, 1, :], wcomb[0:r, i, 1:2], xres[0:r, i, :], MUL, ADD).then_inc(sem["f_sum"], 1)

            def fout(i):
                r = ROWS[i]
                dve.wait_ge(sem["f_std"], i + 1)
                link(V.reciprocal(rstd[0:r, i:i + 1], rstd[0:r, i:i + 1]))
                if i >= 3:
                    dve.wait_ge(sem[f"f_st{i % 3}"], 16 * (i // 3))
                V.scalar_tensor_tensor(fo[i % 3][0:r, :], xres[0:r, i, :], rstd[0:r, i:i + 1], gfin[0:r, :], MUL, MUL).then_inc(sem["f_out"], 1)

            dve.wait_ge(sem["gf_in"], 16)
            for i in range(NT):
                fsum(i)
                if i >= 1:
                    fout(i - 1)
            fout(NT - 1)


_INS = {"x": (TOK, D), "mem": (NM, D), "wk": (D, D), "wv": (D, D), "w_in": (D, 3 * DH), "w_glu": (DH, DH)}


def kernel(**inputs):
    import numpy as _np
    import concourse.bacc as _bacc
    from concourse import mybir as _mybir
    from concourse.bass_utils import run_bass_kernel_spmd as _run

    f32 = _mybir.dt.float32
    a = {k: _np.ascontiguousarray(v) for k, v in inputs.items()}
    nc = _bacc.Bacc("TRN2", target_bir_lowering=False, num_devices=1)
    arrays = {}

    def dram_in(name, array):
        array = _np.ascontiguousarray(array)
        arrays["in_" + name] = array
        return nc.dram_tensor("in_" + name, array.shape, f32, kind="ExternalInput").ap()

    I = {"x": dram_in("x", _np.concatenate([a["x_prompt"].reshape(SEQ, D), a["x_sample"].reshape(NB * DS, D)])),
         "mem": dram_in("mem", a["mem_prompt"].reshape(NM, D)),
         "wk": dram_in("wk", a["xa_w_k"][0]), "wv": dram_in("wv", a["xa_w_v"][0]), "w_in": dram_in("w_in", a["w_in"][0]),
         "w_glu": dram_in("w_glu", a["s5_w_glu"][0]),
         "lam_re": dram_in("lam_re", a["s5_lam_re"].reshape(GP, P)), "lam_im": dram_in("lam_im", a["s5_lam_im"].reshape(GP, P)),
         "log_dt": dram_in("log_dt", a["s5_log_dt"].reshape(GP, 2)),
         "b": [dram_in("b_" + r, a["s5_b_" + r].reshape(GP, P, GC)).rearrange("g p c -> p g c") for r in ("re", "im")],
         "c": [dram_in("c_" + r, a["s5_c_" + r].reshape(GRP * GC, GN)) for r in ("re", "im")],
         "state_s5": [dram_in("state_s5_" + r, a["state_s5_" + r].reshape(NB * GP, P)) for r in ("re", "im")],
         "state_lru_conv": dram_in("state_lru_conv", a["state_lru_conv"].reshape(NB * 3 * CT, P)),
         "w_q": dram_in("w_q", a["xa_w_q"][0]), "w_o": dram_in("w_o", a["xa_w_o"][0]), "w_out": dram_in("w_out", a["w_out"][0]),
         "ck": dram_in("ck", a["cache_mem_k"].reshape(NB * NM, D)), "cv": dram_in("cv", a["cache_mem_v"].reshape(NB * NM, D)),
         "w_group": dram_in("w_group", a["moe_w_group"][0]), "w_expert": dram_in("w_expert", a["moe_w_expert"][0]),
         "w_gate": dram_in("w_gate", a["moe_w_gate"][0]), "w_up": dram_in("w_up", a["moe_w_up"][0]),
         "w_down": dram_in("w_down", a["moe_w_down"][0]), "g_final": dram_in("g_final", a["g_final"].reshape(1, D))}
    for name, rows in VECS:
        I[name] = dram_in(name, a[name].reshape(rows, P))
    for key, name in (("w_a", "lru_w_a"), ("w_x", "lru_w_x")):
        v = dram_in(name, a[name].reshape(CT, 2, 64, 64))
        I[key] = [v[:, h, :, :].rearrange("c i j -> i c j") for h in range(2)]

    shapes = [("y_p", (1, SEQ, D)), ("y_s", (NB, DS, D)), ("mem_k", (1, 1, NM, XH, XD)), ("mem_v", (1, 1, NM, XH, XD)),
              ("s5_re_p", (1, 1, GRP, GN)), ("s5_im_p", (1, 1, GRP, GN)), ("lru_h_p", (1, 1, DH)), ("lru_c_p", (1, 1, 3, DH)),
              ("s5_re_s", (1, NB, GRP, GN)), ("s5_im_s", (1, NB, GRP, GN)), ("lru_h_s", (1, NB, DH)), ("lru_c_s", (1, NB, 3, DH))]
    flat = {"y_p": (SEQ, D), "y_s": (NB * DS, D), "mem_k": (NM, D), "mem_v": (NM, D), "s5_re_p": (GP, P), "s5_im_p": (GP, P),
            "lru_h_p": (CT, P), "lru_c_p": (3 * CT, P), "s5_re_s": (NB * GP, P), "s5_im_s": (NB * GP, P),
            "lru_h_s": (NB * CT, P), "lru_c_s": (NB * 3 * CT, P)}
    O = {n: nc.dram_tensor("out_" + n, flat[n], f32, kind="ExternalOutput").ap() for n, _ in shapes}
    O["s5_p"], O["s5_s"] = [O["s5_re_p"], O["s5_im_p"]], [O["s5_re_s"], O["s5_im_s"]]
    W = {n: nc.dram_tensor("work_" + n, s, f32, kind="Internal").ap()
         for n, s in (("u", (DH, TOK)), ("y", (DH, TOK)), ("klag", (GC, GRP * P)), ("kt", (P, KD * NM)), ("xn", (TOK, D)), ("moe", (2 * TOK, D)))}
    hybrid_layer(nc, I, O, W)
    r = _run(nc, [arrays], core_ids=[0])
    return tuple(r.results[0]["out_" + n].reshape(s) for n, s in shapes)
```
